# Optimizing a Trainium2 kernel written in Bass

```python
import jax, jax.numpy as jnp
from jax import lax
import numpy as np

D_MODEL = 2048
BATCH = 1
SEQ = 512
DEPTH = 1

CHUNK = 64
Q_BLOCK = 128
D_MIX = D_MODEL
FOX_WIDTH = D_MIX // 2
GLA_WIDTH = D_MIX - FOX_WIDTH
FOX_HEAD_DIM = 128
FOX_HEADS = FOX_WIDTH // FOX_HEAD_DIM
GLA_HEADS = 4
GLA_DV = GLA_WIDTH // GLA_HEADS
GLA_DK = GLA_DV // 2
GLA_KEY_WIDTH = GLA_HEADS * GLA_DK
GLA_GATE_RANK = 16
GLA_GATE_TEMP = 16.0
D_FF = 4 * D_MODEL
N_MOD = 6
EPS = 1e-6

IN_SIZES = (FOX_WIDTH, FOX_WIDTH, FOX_WIDTH, FOX_HEADS,
            GLA_KEY_WIDTH, GLA_KEY_WIDTH, GLA_WIDTH, GLA_GATE_RANK, GLA_WIDTH)
IN_OFFSETS = tuple(int(o) for o in np.cumsum(IN_SIZES)[:-1])
D_IN_PROJ = int(sum(IN_SIZES))

kernel_name = "hymba_fox_gla_sandwich_adaln_block"

def rmsnorm(x, g):
    xf = x.astype(jnp.float32)
    y = xf * lax.rsqrt(jnp.mean(xf * xf, axis=-1, keepdims=True) + EPS)
    return (y * g.astype(jnp.float32)).astype(x.dtype)

def head_rmsnorm(x, g):
    xf = x.astype(jnp.float32)
    y = xf * lax.rsqrt(jnp.mean(xf * xf, axis=-1, keepdims=True) + EPS)
    return (y * g.astype(jnp.float32)).astype(x.dtype)

def forgetting_attention(q, k, v, log_f):
    s = q.shape[1]
    scale = FOX_HEAD_DIM ** -0.5
    cum = jnp.transpose(jnp.cumsum(log_f, axis=1), (0, 2, 1))
    neg = jnp.finfo(jnp.float32).min
    outs = []
    for i in range(s // Q_BLOCK):
        q0, q1 = i * Q_BLOCK, (i + 1) * Q_BLOCK
        qb, kb, vb = q[:, q0:q1], k[:, :q1], v[:, :q1]
        logits = jnp.einsum('bqhd,bkhd->bhqk', qb, kb,
                            preferred_element_type=jnp.float32) * scale
        bias = cum[:, :, q0:q1, None] - cum[:, :, None, :q1]
        q_pos = jnp.arange(q0, q1)[:, None]
        k_pos = jnp.arange(q1)[None, :]
        logits = jnp.where(q_pos >= k_pos, logits + bias, neg)
        p = jax.nn.softmax(logits, axis=-1)
        outs.append(jnp.einsum('bhqk,bkhd->bqhd', p.astype(vb.dtype), vb))
    return jnp.concatenate(outs, axis=1)

def gla_chunk_causal(q, k, v, log_a):
    b, s, h, dk = q.shape
    dv = v.shape[-1]
    nc = s // CHUNK
    qc = q.reshape(b, nc, CHUNK, h, dk).astype(jnp.float32) * (dk ** -0.5)
    kc = k.reshape(b, nc, CHUNK, h, dk).astype(jnp.float32)
    vc = v.reshape(b, nc, CHUNK, h, dv).astype(jnp.float32)
    la = log_a.reshape(b, nc, CHUNK, h, dk)
    cum = jnp.cumsum(la, axis=2)
    total = cum[:, :, -1]
    k_dec = kc * jnp.exp(total[:, :, None] - cum)
    u = jnp.einsum('bnchk,bnchv->nbhkv', k_dec, vc)
    decay = jnp.transpose(jnp.exp(total), (1, 0, 2, 3))

    def step(state, inp):
        d_n, u_n = inp
        state = d_n[..., None] * state + u_n
        return state, state

    init = jnp.zeros((b, h, dk, dv), jnp.float32)
    _, states = lax.scan(step, init, (decay, u))
    o = jnp.einsum('bnchk,nbhkv->bnchv', qc, states)
    return o.reshape(b, s, h, dv).astype(v.dtype)

def token_mixer(h, w_in, b_fgate, w_gla_a2, b_gla_a2, g_fox_out, g_gla_out, w_out):
    b, s, _ = h.shape
    proj = h @ w_in
    fq, fk, fv, ff, gq, gk, gv, ga, gr = jnp.split(proj, IN_OFFSETS, axis=-1)

    log_f = jax.nn.log_sigmoid((ff + b_fgate).astype(jnp.float32))
    fox = forgetting_attention(fq.reshape(b, s, FOX_HEADS, FOX_HEAD_DIM),
                               fk.reshape(b, s, FOX_HEADS, FOX_HEAD_DIM),
                               fv.reshape(b, s, FOX_HEADS, FOX_HEAD_DIM), log_f)
    fox = head_rmsnorm(fox, g_fox_out).reshape(b, s, FOX_WIDTH)

    log_a = jax.nn.log_sigmoid((ga @ w_gla_a2 + b_gla_a2).astype(jnp.float32)) / GLA_GATE_TEMP
    gla = gla_chunk_causal(gq.reshape(b, s, GLA_HEADS, GLA_DK),
                           gk.reshape(b, s, GLA_HEADS, GLA_DK),
                           gv.reshape(b, s, GLA_HEADS, GLA_DV),
                           log_a.reshape(b, s, GLA_HEADS, GLA_DK))
    gla = head_rmsnorm(gla, g_gla_out).reshape(b, s, GLA_WIDTH) * jax.nn.silu(gr)

    return jnp.concatenate([fox, gla], axis=-1) @ w_out

def squared_relu_mlp(h, w_mlp_in, w_mlp_out):
    return jnp.square(jax.nn.relu(h @ w_mlp_in)) @ w_mlp_out

def setup_inputs(seed: int = 0) -> dict:
    key = jax.random.key(seed)
    ks = jax.random.split(key, 20)
    nrm = lambda k, shape, s: jax.random.normal(k, shape, jnp.float32) * s
    gain = lambda k, shape: 1.0 + nrm(k, shape, 0.02)
    L = DEPTH
    return {
        "x": nrm(ks[0], (BATCH, SEQ, D_MODEL), 1.0),
        "c": nrm(ks[1], (BATCH, D_MODEL), 1.0),
        "w_ada": nrm(ks[2], (L, D_MODEL, N_MOD * D_MODEL), 0.5 * D_MODEL ** -0.5),
        "b_ada": nrm(ks[3], (L, N_MOD * D_MODEL), 0.02),
        "g_pre_mix": gain(ks[4], (L, D_MODEL)),
        "g_post_mix": gain(ks[5], (L, D_MODEL)),
        "w_in": nrm(ks[6], (L, D_MODEL, D_IN_PROJ), D_MODEL ** -0.5),
        "b_fgate": 2.0 + nrm(ks[7], (L, FOX_HEADS), 0.1),
        "w_gla_a2": nrm(ks[8], (L, GLA_GATE_RANK, GLA_KEY_WIDTH), GLA_GATE_RANK ** -0.5),
        "b_gla_a2": nrm(ks[9], (L, GLA_KEY_WIDTH), 0.02),
        "g_fox_out": gain(ks[10], (L, FOX_HEADS, FOX_HEAD_DIM)),
        "g_gla_out": gain(ks[11], (L, GLA_HEADS, GLA_DV)),
        "w_out": nrm(ks[12], (L, D_MIX, D_MODEL), D_MIX ** -0.5),
        "g_pre_mlp": gain(ks[13], (L, D_MODEL)),
        "g_post_mlp": gain(ks[14], (L, D_MODEL)),
        "w_mlp_in": nrm(ks[15], (L, D_MODEL, D_FF), D_MODEL ** -0.5),
        "w_mlp_out": nrm(ks[16], (L, D_FF, D_MODEL), D_FF ** -0.5),
    }

def reference(x, c, w_ada, b_ada, g_pre_mix, g_post_mix, w_in, b_fgate, w_gla_a2,
              b_gla_a2, g_fox_out, g_gla_out, w_out, g_pre_mlp, g_post_mlp,
              w_mlp_in, w_mlp_out):
    c_act = jax.nn.silu(c)
    for i in range(DEPTH):
        mod = (c_act @ w_ada[i] + b_ada[i])[:, None, :]
        shift_m, scale_m, gate_m, shift_f, scale_f, gate_f = jnp.split(mod, N_MOD, axis=-1)

        h = rmsnorm(x, g_pre_mix[i]) * (1.0 + scale_m) + shift_m
        y = token_mixer(h, w_in[i], b_fgate[i], w_gla_a2[i], b_gla_a2[i],
                        g_fox_out[i], g_gla_out[i], w_out[i])
        x = x + gate_m * rmsnorm(y, g_post_mix[i])

        h = rmsnorm(x, g_pre_mlp[i]) * (1.0 + scale_f) + shift_f
        y = squared_relu_mlp(h, w_mlp_in[i], w_mlp_out[i])
        x = x + gate_f * rmsnorm(y, g_post_mlp[i])
    return x


_drawn_inputs = setup_inputs


def setup_inputs(seed=0):
    import zlib

    import numpy as np

    out = dict(_drawn_inputs(seed))
    spreads = {}
    factors = {'g_pre_mix': 6.624,
     'g_post_mix': 21.421,
     'b_fgate': 6.149,
     'b_gla_a2': 8.0,
     'g_fox_out': 200.0,
     'g_gla_out': 70.855,
     'g_pre_mlp': 84.828,
     'g_post_mlp': 106.097}
    for name, (base, spread) in spreads.items():
        noise = np.random.default_rng([zlib.crc32(name.encode()), seed]).standard_normal(out[name].shape)
        drawn = base * np.exp(spread * noise) if base else spread * noise
        out[name] = __import__('jax').numpy.asarray(drawn.astype(out[name].dtype))
    for name, factor in factors.items():
        out[name] = (out[name] * factor).astype(out[name].dtype)
    return out
```

```python
from contextlib import ExitStack

import numpy as np

import concourse.bass as bass
from concourse import mybir

F32 = mybir.dt.float32
F32R = mybir.dt.float32r
ALU = mybir.AluOpType
ACT = mybir.ActivationFunctionType
AX_X = mybir.AxisListType.X

P = 128
KIB = 1024


def build_block(nc, x, c, w_ada, b_ada, g_pre_mix, g_post_mix, w_in, b_fgate, w_gla_a2, b_gla_a2,
                g_fox_out, g_gla_out, w_out, g_pre_mlp, g_post_mlp, w_mlp_in, w_mlp_out, out):
    _, SEQ, D = x.shape
    KT = D // P
    TB = SEQ // P
    FOX_HEADS, FOX_DIM = g_fox_out.shape[1:]
    GLA_HEADS, GLA_DV = g_gla_out.shape[1:]
    RANK, GLA_KEYS = w_gla_a2.shape[1:]
    GLA_DK = GLA_KEYS // GLA_HEADS
    FOX_WIDTH = FOX_HEADS * FOX_DIM
    GLA_WIDTH = GLA_HEADS * GLA_DV
    D_FF = w_mlp_in.shape[2]
    CHUNK = 64
    NCH = SEQ // CHUNK
    EPS = 1e-6
    GATE_TEMP = 16.0
    MASKED = float(np.finfo(np.float32).min)
    assert FOX_DIM == P and GLA_DK == P and GLA_DV == 2 * P and SEQ == 512 and KT == 16

    FF_COL = 3 * FOX_WIDTH
    GQ_COL = FF_COL + FOX_HEADS
    GK_COL = GQ_COL + GLA_KEYS
    GV_COL = GK_COL + GLA_KEYS
    GA_COL = GV_COL + GLA_WIDTH
    GR_COL = GA_COL + RANK

    TILES = 6
    FOX_GROUPS = FOX_HEADS // 2
    GROUPS = FOX_GROUPS + GLA_HEADS
    QA, QB, KA, KB, VA, VB = range(6)
    GQ, GK, GV0, GV1, GR0, GR1 = range(6)
    MM_G = KT // 2
    MM_O = KT // 4
    CG = D // 512
    FBLK = 1024
    FT = FBLK // P
    FBS = D_FF // FBLK
    M_OUT = GROUPS * MM_G
    M_MLP = M_OUT + CG * MM_O
    MM_F = 2 * MM_O + CG * 2
    GROUP_DMAS = 4
    RAW_OUT = 16 * GROUP_DMAS * (GROUPS * MM_G // 2)
    RAW_MLP = RAW_OUT + 16 * (CG * MM_O // 2)

    SHIFT_M, SCALE_M, GATE_M, SHIFT_F, SCALE_F, GATE_F = [n * D for n in range(6)]
    Q_FOX = KT
    Q_GLA = Q_FOX + 3 * FOX_GROUPS
    Q_GF = Q_GLA + 3 * GLA_HEADS

    x_t = x[0].rearrange("(t p) d -> p t d", p=P)
    out_t = out[0].rearrange("(t p) d -> p t d", p=P)
    w_ada_t = w_ada[0].rearrange("(k p) n -> p k n", p=P)
    w_in_t = w_in[0].rearrange("(k p) n -> p k n", p=P)
    w_out_t = w_out[0].rearrange("(k p) n -> p k n", p=P)
    w_m1_t = w_mlp_in[0].rearrange("(k p) n -> p k n", p=P)
    w_m2_t = w_mlp_out[0].rearrange("(k p) n -> p k n", p=P)

    with ExitStack() as ctx:
        base = 16512
        R_A = base
        R_B = R_A + 64 * KIB
        R_C = R_B + 32 * KIB
        R_G = R_C + 48 * KIB
        R_T = R_G + 12 * KIB
        R_AD = R_G + 32 * KIB
        R_GG = R_AD + 16 * KIB
        R_K = R_GG + 8 * KIB

        def at(name, shape, offset, dt=F32):
            return nc.alloc_sbuf_tensor_at(name, shape, dt, offset=offset)

        in_hi = at("in_hi", [P, KT, SEQ], R_A, F32R)
        in_lo = at("in_lo", [P, KT, SEQ], R_A + 32 * KIB, F32R)
        in_tmp = at("in_tmp", [P, KT, SEQ], R_A + 32 * KIB)
        x_raw = at("x_raw", [P, TB, D], R_A + 32 * KIB)
        x_junk = at("x_junk", [P, D], R_A)
        x1_end = at("x1_end", [P, TB, D], R_A)
        o_junk = at("o_junk", [P, TB, 512], R_A + 32 * KIB)
        xn_t = at("xn_t", [P, KT, SEQ], R_B)
        cat = at("cat", [P, KT, SEQ], R_B)
        x_res = at("x_res", [P, TB, D], R_B)
        hid_hi = at("hid_hi", [P, FT, SEQ], R_B, F32R)
        hid_lo = at("hid_lo", [P, FT, SEQ], R_B + 16 * KIB, F32R)
        hid_tmp = at("hid_tmp", [P, FT, SEQ], R_B + 16 * KIB)
        w_raw = [at(f"w_raw{s}", [P, 2048], R_C + 8 * KIB * s) for s in range(2)]
        w_hi = [at(f"w_hi{s}", [P, 2048], R_C + 8 * KIB * (2 + s), F32R) for s in range(2)]
        w_lo = [at(f"w_lo{s}", [P, 2048], R_C + 8 * KIB * (4 + s), F32R) for s in range(2)]
        grp = at("grp", [P, TILES, SEQ], R_G)
        y = at("y", [P, TB, D], R_G)
        ada1 = [at(f"ada1{u}", [P, KT, P], R_G + 8 * KIB * u) for u in range(2)]
        rows_a = at("rows_a", [6 * KT, P], R_G + 16 * KIB)
        rows_c = at("rows_c", [KT, P], R_B)
        rows_b = at("rows_b", [20, P], R_G + 16 * KIB + 512)
        wm_raw = at("wm_raw", [P, KT, 40], R_T + 8 * KIB)
        wm_hi = at("wm_hi", [P, KT, 40], R_GG, F32R)
        wm_lo = at("wm_lo", [P, KT, 40], R_G + 17 * KIB, F32R)
        f_z = at("f_z", [40, SEQ], R_T + 4 * KIB)
        f_a = at("f_a", [40, SEQ], R_T + 6 * KIB)
        cumb = [at(f"cumb{n}", [P, SEQ], R_T + 2 * KIB * n) for n in range(2)]
        bias = at("bias", [P, SEQ], R_T + 4 * KIB)
        logit = at("logit", [P, SEQ], R_T + 6 * KIB)
        prob = at("prob", [P, SEQ], R_T + 8 * KIB)
        prob_t = at("prob_t", [P, SEQ], R_T + 10 * KIB)
        fv_tok = at("fv_tok", [P, 2, TB, P], R_T + 12 * KIB)
        f_o = at("f_o", [P, P], R_T + 16 * KIB)
        f_junk = at("f_junk", [P, P], R_T + 16 * KIB + 512)
        neg_max, row_max, row_sum, row_inv, f_ms, f_r = [
            at(name, [P, 8], R_T + 17 * KIB + 32 * n) for n, name in enumerate(
                ("neg_max", "row_max", "row_sum", "row_inv", "f_ms", "f_r"))]
        causal = at("causal", [P, P], R_T + 17 * KIB + 256)
        states = at("states", [P, NCH, GLA_DV], R_T)
        g_z = at("g_z", [P, SEQ], R_T)
        g_e = at("g_e", [P, SEQ], R_T + 2 * KIB)
        g_cum = at("g_cum", [P, NCH, CHUNK], R_T + 4 * KIB)
        g_dif = at("g_dif", [P, NCH, CHUNK], R_T + 6 * KIB)
        sig = grp[:, GV0:GV1 + 1, :]
        g_junk = at("g_junk", [P, GLA_DV], R_T + 4 * KIB)
        gv_tok = at("gv_tok", [P, TB, GLA_DV], R_T + 8 * KIB)
        kd_tok = at("kd_tok", [P, TB, P], R_T + 12 * KIB)
        g_o = at("g_o", [P, TB, GLA_DV], R_T + 14 * KIB)
        chunk_on = at("chunk_on", [P, SEQ], R_T + 18 * KIB)
        ada0 = [at(f"ada0{u}", [P, KT, P], R_AD + 8 * KIB * u) for u in range(2)]
        gg = at("gg", [P, D], R_GG)

        k_at = [R_K]

        def small(name, shape):
            t = at(name, shape, k_at[0])
            size = 4
            for n in shape[1:]:
                size *= n
            k_at[0] += (size + 31) // 32 * 32
            return t

        ident = small("ident", [P, P])
        ones = small("ones", [P, P])
        acc = [small("acc0", [P, 2 * P]), at("acc1", [P, 2 * P], R_T + 16 * KIB)]
        bg_bc = small("bg_bc", [P, 2, 2 * P])
        cols_a = small("cols_a", [P, 6 * KT])
        cols_b = small("cols_b", [P, 20])
        mod_a = small("mod_a", [P, KT])
        mod_b = small("mod_b", [P, KT])
        c_act = small("c_act", [P, KT])
        ga_t = small("ga_t", [RANK, SEQ])
        a2h = small("a2h", [RANK, P])
        b_fg = small("b_fg", [40, 1])
        cumq = small("cumq", [P, TB, FOX_HEADS])
        neg_half = small("neg_half", [P, 16])
        ss = small("ss", [P, 16])
        ms = small("ms", [P, 16])
        rstd = small("rstd", [P, 16])
        ss4 = small("ss4", [P, 4])
        decay = small("decay", [P, NCH])
        assert k_at[0] <= nc.sbuf_usable_end

        C_GPRE, C_SHM, C_SCM, C_SHF, C_SCF, C_GPRE2 = [KT * n for n in range(6)]
        B_A2, B_GFOX, B_GGLA = 0, GLA_HEADS, GLA_HEADS + FOX_HEADS

        bank = [ctx.enter_context(nc.psum_tensor(f"bank{b}", [P, 512], F32)) for b in range(8)]
        BA, BB = bank[6], bank[7]

        cum_dram = nc.dram_tensor("cum_scratch", (FOX_HEADS, SEQ), F32, kind="Internal").ap()
        x1_dram = nc.dram_tensor("x1_scratch", (SEQ, D), F32, kind="Internal").ap()
        x1_t = x1_dram.rearrange("(t p) d -> p t d", p=P)

        def sem(name):
            return ctx.enter_context(nc.semaphore(name))

        x_in = [sem(f"x_in{t}") for t in range(TB)]
        rows_in = sem("rows_in")
        c_in = sem("c_in")
        bfg_in = sem("bfg_in")
        wm_in = sem("wm_in")
        w_in_s = [sem("w_in0"), sem("w_in1")]
        ada_in = [[sem(f"ada_in{b}{u}") for u in range(2)] for b in range(2)]
        bg_in = sem("bg_in")
        a2_in = sem("a2_in")
        cum_out = sem("cum_out")
        cumb_in = sem("cumb_in")
        xres_in = [sem(f"xres_in{t}") for t in range(TB)]
        x1_out = sem("x1_out")
        x1_in = [sem(f"x1_in{t}") for t in range(TB)]
        out_done = sem("out_done")
        hi_done = sem("hi_done")
        lo_done = sem("lo_done")
        w_used = sem("w_used")
        tile_sum = sem("tile_sum")
        ev_act = sem("ev_act")
        ev_dve = sem("ev_dve")
        consts = sem("consts")
        rows_tr = sem("rows_tr")
        c_tr = sem("c_tr")
        cols_ready = sem("cols_ready")
        ce_ready = sem("ce_ready")
        c_ready = sem("c_ready")
        x_ss = sem("x_ss")
        x_rstd = sem("x_rstd")
        xn_ready = sem("xn_ready")
        x_tr = sem("x_tr")
        xt_act = sem("xt_act")
        xt_dve = sem("xt_dve")
        wm_zero = sem("wm_zero")
        wm_hid = sem("wm_hid")
        wm_lod = sem("wm_lod")
        misc_sum = sem("misc_sum")
        fz_abs = sem("fz_abs")
        fz_ln = sem("fz_ln")
        ga_ready = sem("ga_ready")
        cum_ready = sem("cum_ready")
        cumq_tr = sem("cumq_tr")
        cumq_ready = sem("cumq_ready")
        ada_mul = [sem("ada_mul_act"), sem("ada_mul_pool")]
        ada_acc = [sem("ada_acc0"), sem("ada_acc1")]
        ada_sum = sem("ada_sum")
        ada_col = sem("ada_col")
        mod_tmp = sem("mod_tmp")
        mod_hi = sem("mod_hi")
        mod_lo = sem("mod_lo")
        fvt, fvc, fqk, fbr, fsm, fexp, fpt, fptc, fpv, fob, fss, frn, fon = [
            sem(n) for n in ("fox_v_tr", "fox_v_tok", "fox_qk", "fox_bias", "fox_max",
                             "fox_exp", "fox_p_tr", "fox_p_tok", "fox_pv", "fox_out", "fox_ss",
                             "fox_rstd", "fox_norm")]
        (gz, gaz, gln, gdf, gde, gkd, gvt, gvc, gkt, gkc, gu, gst, go, goc, gss, grn, gon, gre, gsg,
         gt, gcat) = [
            sem(n) for n in ("gla_z", "gla_abs", "gla_ln", "gla_cum", "gla_decay", "gla_kd", "gla_v_tr",
                             "gla_v_tok", "gla_k_tr", "gla_k_tok", "gla_u", "gla_state", "gla_o",
                             "gla_o_tok", "gla_ss", "gla_rstd", "gla_norm", "gla_sig_e", "gla_sig",
                             "gla_o_tr", "gla_cat")]
        cat_hi = sem("cat_hi")
        cat_lo = sem("cat_lo")
        y_sum = sem("y_sum")
        y_sq = sem("y_sq")
        y_mul = sem("y_mul")
        y_rstd = sem("y_rstd")
        y_gate = sem("y_gate")
        x1_ready = sem("x1_ready")
        x1_pool = sem("x1_pool")
        x1_ss = sem("x1_ss")
        x1_sq = sem("x1_sq")
        xn2_dve = sem("xn2_dve")
        x1_rstd = sem("x1_rstd")
        xn2_ready = sem("xn2_ready")
        x1_part = sem("x1_part")
        h_sum = sem("h_sum")
        h_relu = sem("h_relu")
        h_sq = sem("h_sq")
        h_hi = sem("h_hi")
        h_lo = sem("h_lo")
        y2_sum = sem("y2_sum")
        y2_add = sem("y2_add")
        o_sq = sem("o_sq")
        o_mul = sem("o_mul")
        o_mul_last = sem("o_mul_last")
        o_ss = sem("o_ss")
        o_rstd = sem("o_rstd")
        o_part = sem("o_part")
        o_ready = sem("o_ready")
        o_pool = sem("o_pool")

        def arrived_group(r, mm):
            return 16 * GROUP_DMAS * (r * (MM_G // 2) + mm // 2 + 1)

        def arrived_out(cg, mm):
            return RAW_OUT + 16 * (cg * (MM_O // 2) + mm // 2 + 1)

        def arrived_mlp(fb, mm):
            return RAW_MLP + 16 * (fb * (MM_F // 2) + mm // 2 + 1)

        def group_view(t):
            return t[:, 0:2 * TILES * P].rearrange("p (k n) -> p k n", k=2)

        def wide_view(t):
            return t[:, :].rearrange("p (k n) -> p k n", k=4)

        block = ctx.enter_context(nc.Block())

        @block.sync
        def _(sp):
            def slot_free(m):
                sp.wait_ge(hi_done, m - 1)
                sp.wait_ge(lo_done, m - 1)

            def load_fox(r, mm, wait=True):
                if wait:
                    slot_free(r * MM_G + mm)
                dst = group_view(w_raw[mm % 2])
                for k in range(2):
                    src = w_in_t[:, 2 * mm + k, 0:3 * FOX_WIDTH].rearrange("p (s n) -> p s n", s=3)
                    to = dst[:, k, :].rearrange("p (s n) -> p s n", s=3)
                    for part in (slice(0, 2), slice(2, 3)):
                        sp.dma_start(to[:, part, :], src[:, part, bass.ds(r * 2 * P, 2 * P)])\
                            .then_inc(w_in_s[mm % 2], 16)

            def load_gla(h, mm):
                slot_free((FOX_GROUPS + h) * MM_G + mm)
                dst = group_view(w_raw[mm % 2])
                k = slice(2 * mm, 2 * mm + 2)
                for t, col, width in ((GQ, GQ_COL, GLA_DK), (GK, GK_COL, GLA_DK), (GV0, GV_COL, GLA_DV),
                                      (GR0, GR_COL, GLA_DV)):
                    sp.dma_start(dst[:, :, t * P:t * P + width],
                                 w_in_t[:, k, bass.ds(h * width + col, width)]).then_inc(w_in_s[mm % 2], 16)

            def load_out(cg, mm):
                slot_free(M_OUT + cg * MM_O + mm)
                sp.dma_start(wide_view(w_raw[mm % 2]), w_out_t[:, 4 * mm:4 * mm + 4, cg * 512:cg * 512 + 512])\
                    .then_inc(w_in_s[mm % 2], 16)

            def load_m1(fb, half, mm):
                slot_free(M_MLP + fb * MM_F + half * MM_O + mm)
                sp.dma_start(wide_view(w_raw[mm % 2]),
                             w_m1_t[:, 4 * mm:4 * mm + 4, bass.ds(fb * FBLK + half * 512, 512)])\
                    .then_inc(w_in_s[mm % 2], 16)

            def load_m2(fb, cg, mm):
                slot_free(M_MLP + fb * MM_F + 2 * MM_O + cg * 2 + mm)
                sp.dma_start(wide_view(w_raw[mm % 2]),
                             w_m2_t[:, bass.ds(fb * FT + 4 * mm, 4), cg * 512:cg * 512 + 512])\
                    .then_inc(w_in_s[mm % 2], 16)

            def load_ada(summed, col_a, col_b, b):
                for u, col in enumerate((col_a, col_b)):
                    if summed is not None:
                        sp.wait_ge(ada_acc[u], summed)
                    sp.dma_start((ada0, ada1)[b][u][:, :, :], w_ada_t[:, :, bass.ds(col, P)])\
                        .then_inc(ada_in[b][u], 16)

            def load_mod_f(q, k):
                load_ada(q, k * P + SCALE_F, k * P + SHIFT_F, 0)

            def load_gate(q, k, col, g_post):
                load_ada(q, k * 2 * P + col, k * 2 * P + col + P, 0)
                sp.wait_ge(ada_col, q)
                sp.dma_start(bg_bc[:, 0, :], b_ada[0:1, bass.ds(k * 2 * P + col, 2 * P)].to_broadcast([P, 2 * P]))\
                    .then_inc(bg_in, 16)
                sp.dma_start(bg_bc[:, 1, :], g_post[0:1, bass.ds(k * 2 * P, 2 * P)].to_broadcast([P, 2 * P]))\
                    .then_inc(bg_in, 16)

            def as_rows(dst, src, done):
                sp.dma_start(dst, src.rearrange("o (k p) -> (o k) p", p=P)).then_inc(done, 16)

            def load_ada_m(q):
                load_ada(q - 1 if q >= 2 else None, q * P + SCALE_M, q * P + SHIFT_M, q % 2)

            as_rows(rows_c[:, :], c[0:1, :], c_in)
            load_ada_m(0)
            load_ada_m(1)
            for n, src in enumerate((g_pre_mix[0:1, :], b_ada[0:1, SHIFT_M:SHIFT_M + D],
                                     b_ada[0:1, SCALE_M:SCALE_M + D], b_ada[0:1, SHIFT_F:SHIFT_F + D],
                                     b_ada[0:1, SCALE_F:SCALE_F + D], g_pre_mlp[0:1, :])):
                as_rows(rows_a[n * KT:(n + 1) * KT, :], src, rows_in)
            as_rows(rows_b[B_A2:B_GFOX, :], b_gla_a2, rows_in)
            sp.dma_start(rows_b[B_GFOX:B_GGLA, :], g_fox_out[0]).then_inc(rows_in, 16)
            sp.dma_start(rows_b[B_GGLA:20, :], g_gla_out[0].rearrange("h (k p) -> (h k) p", p=P)).then_inc(rows_in, 16)
            for t in range(TB):
                sp.dma_start(x_raw[:, t, :], x_t[:, t, :]).then_inc(x_in[t], 16)
            sp.wait_ge(wm_zero, 1)
            sp.dma_start(wm_raw[:, :, 0:RANK], w_in_t[:, :, GA_COL:GA_COL + RANK]).then_inc(wm_in, 16)
            sp.dma_start(wm_raw[:, :, 32:32 + FOX_HEADS], w_in_t[:, :, FF_COL:FF_COL + FOX_HEADS]).then_inc(wm_in, 16)
            sp.dma_start(b_fg[32:40, :], b_fgate.rearrange("o h -> h o")).then_inc(bfg_in, 16)
            load_fox(0, 0, wait=False)
            load_ada_m(2)
            load_fox(0, 1, wait=False)
            for q in range(3, KT):
                load_ada_m(q)
                if q % 2 and q < KT - 1:
                    load_fox(0, (q + 1) // 2)

            def load_cumb(f):
                sp.wait_ge(ev_act, 3 * f + 1)
                for n in range(2):
                    sp.dma_start(cumb[n][:, :], cum_dram[bass.ds(2 * f + n, 1), :].to_broadcast([P, SEQ]))\
                        .then_inc(cumb_in, 16)

            ADA_AT = {1: 0, 4: 1, 6: 2}

            with sp.Fori(1, FOX_GROUPS) as r:
                for mm in range(MM_G):
                    load_fox(r, mm)
                    if mm == 1:
                        sp.wait_ge(cum_out, 16)
                        load_cumb(r - 1)
                    if mm in ADA_AT:
                        k = (r - 1) * 3 + ADA_AT[mm]
                        load_mod_f(k + Q_FOX, k)
            for mm in range(MM_G):
                load_gla(0, mm)
                if mm == 0:
                    load_cumb(FOX_GROUPS - 1)
                if mm in ADA_AT:
                    k = 3 * (FOX_GROUPS - 1) + ADA_AT[mm]
                    load_mod_f(k + Q_FOX, k)
            with sp.Fori(0, GLA_HEADS - 1) as h:
                for mm in range(MM_G):
                    load_gla(h + 1, mm)
                    if mm == 0:
                        sp.wait_ge(ev_act, 3 * (FOX_GROUPS + h) + 1)
                        sp.dma_start(a2h[:, :], w_gla_a2[0, :, bass.ds(h * P, P)]).then_inc(a2_in, 16)
                    if mm in ADA_AT:
                        j = ADA_AT[mm]
                        if j == 0:
                            load_mod_f(h * 3 + Q_GLA, h + 3 * FOX_GROUPS)
                        else:
                            load_gate(h * 3 + (Q_GLA + j), h * 2 + (j - 1), GATE_M, g_post_mix)
            sp.wait_ge(gz, GLA_HEADS - 1)
            sp.dma_start(a2h[:, :], w_gla_a2[0, :, (GLA_HEADS - 1) * P:GLA_HEADS * P]).then_inc(a2_in, 16)
            for cg in range(CG):
                for mm in range(MM_O):
                    load_out(cg, mm)
                    if cg == 0 and mm == 0:
                        load_mod_f(Q_GF - 3, KT - 1)
                    if cg in (1, 2) and mm == 0:
                        load_gate(Q_GF - 3 + cg, KT // 2 - 3 + cg, GATE_M, g_post_mix)
                if cg == 1:
                    sp.wait_ge(cat_hi, KT)
                    sp.wait_ge(cat_lo, KT)
                    for t in range(TB):
                        sp.dma_start(x_res[:, t, :], x_t[:, t, :]).then_inc(xres_in[t], 16)
            with sp.Fori(0, FBS) as fb:
                for half in range(2):
                    for mm in range(MM_O):
                        load_m1(fb, half, mm)
                        if half == 0 and mm == 2:
                            load_gate(fb + Q_GF, fb, GATE_F, g_post_mlp)
                for cg in range(CG):
                    for mm in range(2):
                        load_m2(fb, cg, mm)
            sp.wait_ge(x1_out, 16 * TB)
            sp.wait_ge(w_used, M_MLP + (FBS - 1) * MM_F + 2 * MM_O)
            for t in range(TB):
                sp.dma_start(x1_end[:, t, :], x1_t[:, t, :]).then_inc(x1_in[t], 16)
            for t in range(TB):
                if t < TB - 1:
                    sp.wait_ge(o_ready, t + 1)
                else:
                    sp.wait_ge(o_pool, 1)
                sp.dma_start(out_t[:, t, :], x1_end[:, t, :]).then_inc(out_done, 16)
            sp.wait_ge(out_done, 16 * TB)

        @block.tensor
        def _(pe):
            def split_mm(dst, a, b, start, stop):
                pe.matmul(dst, a[0], b[0], start=start, stop=False)
                pe.matmul(dst, a[0], b[1], start=False, stop=False)
                return pe.matmul(dst, a[1], b[0], start=False, stop=stop)

            def group_steps(r, first, slot, misc_step=None):
                for k in range(KT):
                    s, m = (k // 2) % 2, r * MM_G + k // 2
                    hi, lo = group_view(w_hi[s])[:, k % 2, :], group_view(w_lo[s])[:, k % 2, :]
                    if first:
                        slot(2 * k)
                    if k % 2 == 0:
                        pe.wait_ge(hi_done, m + 1)
                        pe.wait_ge(lo_done, m + 1)
                    if first:
                        pe.wait_ge(mod_lo, k + 1)
                        misc_step(k)
                    for b in range(TILES):
                        if k == 0 and not first:
                            pe.wait_ge((ev_act, ev_dve)[b % 2], r * 3 - 2 + b // 2)
                        cols = slice(b * P, b * P + P)
                        last = split_mm(bank[b][:, :], (hi[:, cols], lo[:, cols]),
                                        (in_hi[:, k, :], in_lo[:, k, :]), k == 0, k == KT - 1)
                        if k == KT - 1 and b < TILES - 1:
                            last.then_inc(tile_sum, 1)
                        if b == TILES - 1 and k % 2:
                            last.then_inc(w_used, 1)
                        if not first and b == 2:
                            slot(2 * k)
                    if not first:
                        slot(2 * k + 1)

            def ada_columns(q, dst, a=0):
                pe.wait_ge(ada_acc[0], q + 1)
                pe.wait_ge(ada_acc[1], q + 1)
                pe.matmul(dst[:, 0:1], acc[a][:, 0:P], ones[:, 0:1], start=True, stop=True)
                pe.matmul(dst[:, 1:2], acc[a][:, P:2 * P], ones[:, 0:1], start=True, stop=True).then_inc(ada_sum, 1)

            def ada_rows(q, dst):
                pe.wait_ge(ada_acc[0], q + 1)
                pe.wait_ge(ada_acc[1], q + 1)
                pe.matmul(dst[:, 0:2 * P], ones[:, :], acc[0][:, :], start=True, stop=True).then_inc(ada_sum, 1)

            def fox_slot(s, f):
                if s == 0:
                    pe.wait_ge(ev_act, 3 * f + 3)
                    pe.wait_ge(ev_dve, 3 * f + 3)
                    for t in range(TB):
                        last = pe.transpose(BB[:, t * P:t * P + P], grp[:, VA, t * P:t * P + P], ident[:, :])
                    last.then_inc(fvt, 1)
                if s == 1:
                    pe.wait_ge(fsm, 8 * f + 1)
                    for t in range(TB):
                        last = pe.transpose(BA[:, t * P:t * P + P], grp[:, VB, t * P:t * P + P], ident[:, :])
                    last.then_inc(fvt, 1)
                if s % 3 == 0 and s // 3 < 8:
                    j = s // 3
                    i = j % TB
                    if j:
                        pe.wait_ge(fsm, 8 * f + j)
                    if j == 1:
                        pe.wait_ge(fvc, 2 * f + 2)
                    if j == 0:
                        pe.wait_ge(ada_col, 3 * f + Q_FOX)
                    q_tile, k_tile = (QA, KA) if j < TB else (QB, KB)
                    pe.matmul(BA[:, 0:(i + 1) * P], grp[:, q_tile, i * P:i * P + P], grp[:, k_tile, 0:(i + 1) * P],
                              start=True, stop=True).then_inc(fqk, 1)
                if s % 3 == 2 and s // 3 < 8:
                    j = s // 3
                    pe.wait_ge(fexp, 8 * f + j + 1)
                    if j == 0:
                        pe.wait_ge(fvc, 2 * f + 1)
                    else:
                        pe.wait_ge(fob, 9 * f + j)
                    for t in range(j % TB + 1):
                        last = pe.transpose(BB[:, t * P:t * P + P], prob[:, t * P:t * P + P], ident[:, :])
                    last.then_inc(fpt, 1)
                if s % 3 == 1 and 4 <= s <= 25:
                    j = (s - 4) // 3
                    i = j % TB
                    pe.wait_ge(fptc, 8 * f + j + 1)
                    if j == 0:
                        pe.wait_ge(fvc, 2 * f + 2)
                    else:
                        fox_out_transpose(f, j - 1)
                    for t in range(i + 1):
                        last = pe.matmul(BB[:, 0:P], prob_t[:, t * P:t * P + P], fv_tok[:, j // TB, t, :],
                                         start=(t == 0), stop=(t == i))
                    last.then_inc(fpv, 1)
                if s == 28:
                    pe.wait_ge(fob, 9 * f + 8)
                    fox_out_transpose(f, 7).then_inc(fpv, 1)

            def fox_out_transpose(f, j):
                pe.wait_ge(fon, 8 * f + j + 1)
                return pe.transpose(BB[:, P:2 * P], f_o[:, :], ident[:, :])

            def gla_slot(s, h, ada, last_head=False):
                if s == 0:
                    pe.wait_ge(ev_act, 3 * (h + FOX_GROUPS) + 3)
                    pe.wait_ge(ev_dve, 3 * (h + FOX_GROUPS) + 3)
                    pe.wait_ge(a2_in, 16 * (h + 1))
                    pe.wait_ge(fob, 9 * FOX_GROUPS)
                    pe.wait_ge(fsm, 8 * FOX_GROUPS)
                    pe.wait_ge(ada_col, ada)
                    pe.matmul(BA[:, :], a2h[:, :], ga_t[:, :], start=True, stop=True).then_inc(gz, 1)
                if s in (1, 3):
                    if s == 3:
                        pe.wait_ge(gvc, 2 * h + 1)
                    for t in range(TB):
                        last = pe.transpose(BB[:, t * P:t * P + P], grp[:, GV0 + s // 2, t * P:t * P + P], ident[:, :])
                    last.then_inc(gvt, 1)
                if s == 7:
                    pe.wait_ge(gkd, h + 1)
                    for t in range(TB):
                        last = pe.transpose(BA[:, t * P:t * P + P], g_e[:, t * P:t * P + P], ident[:, :])
                    last.then_inc(gkt, 1)
                if s == 12:
                    pe.wait_ge(gst, 2 * h + 1)
                    ada_columns(ada, BB)
                if s in (10, 13):
                    if s == 10:
                        pe.wait_ge(gkc, h + 1)
                    else:
                        pe.wait_ge(ada_col, ada + 1)
                    for n in range(4):
                        t, rows = (n + 4 * (s == 13)) // 2, slice(CHUNK * (n % 2), CHUNK * (n % 2) + CHUNK)
                        last = pe.matmul((BA, BB)[n % 2][:, (n // 2) * GLA_DV:(n // 2 + 1) * GLA_DV],
                                         kd_tok[rows, t, :], gv_tok[rows, t, :], start=True, stop=True)
                    last.then_inc(gu, 1)
                if s in (16, 17):
                    if s == 16:
                        pe.wait_ge(gst, 2 * h + 2)
                    for n in range(4):
                        ch = n + 4 * (s == 17)
                        rows = slice(CHUNK * (n % 2), CHUNK * (n % 2) + CHUNK)
                        last = pe.matmul((BA, BB)[s - 16][rows, (n // 2) * GLA_DV:(n // 2 + 1) * GLA_DV],
                                         grp[:, GQ, ch * CHUNK:ch * CHUNK + CHUNK], states[:, ch, :],
                                         start=True, stop=True)
                    last.then_inc(go, 1)
                if s == 20 and not last_head:
                    pe.wait_ge(goc, 2 * h + 1)
                    ada_rows(ada + 1, BA)
                if s in (23, 24):
                    if s == 23:
                        pe.wait_ge(gon, h + 1)
                        if not last_head:
                            pe.wait_ge(ada_col, ada + 2)
                    half = s - 23
                    for t in range(TB):
                        last = pe.transpose((BA, BB)[half][:, t * P:t * P + P],
                                            g_o[:, t, half * P:half * P + P], ident[:, :])
                    last.then_inc(gt, 1)
                if s == 30 and not last_head:
                    pe.wait_ge(gcat, 2 * h + 1)
                    ada_rows(ada + 2, BA)

            pe.wait_ge(consts, 1)
            pe.wait_ge(c_in, 16)
            pe.transpose(BB[:, 0:KT], rows_c[:, :], ident[0:KT, 0:KT]).then_inc(c_tr, 1)
            pe.wait_ge(rows_in, 16 * 9)
            pe.transpose(BA[:, 0:6 * KT], rows_a[:, :], ident[0:6 * KT, 0:6 * KT])
            pe.transpose(BA[:, 128:148], rows_b[:, :], ident[0:20, 0:20]).then_inc(rows_tr, 1)
            for k in range(KT):
                if k == 0:
                    pe.wait_ge(xn_ready, TB)
                if k >= TILES:
                    pe.wait_ge((xt_act, xt_dve)[k % 2], (k - TILES) // 2 + 1)
                for t in range(TB):
                    last = pe.transpose(bank[k % TILES][:, t * P:t * P + P], x_raw[:, t, k * P:k * P + P], ident[:, :])
                last.then_inc(x_tr, 1)

            def start_slot(s):
                if s == 0:
                    pe.wait_ge(xt_act, KT // 2)
                    pe.wait_ge(xt_dve, KT // 2)
                    pe.wait_ge(cols_ready, 1)
                    pe.wait_ge(c_ready, 1)
                    ada_columns(0, BA[:, 0:2], 0)
                if s % 2 == 0 and s // 2 + 1 < KT:
                    q = s // 2 + 1
                    pe.wait_ge(ada_col, q)
                    ada_columns(q, BA[:, 0:2], q % 2)

            def misc_step(k):
                if k == 0:
                    pe.wait_ge(wm_hid, 1)
                    pe.wait_ge(wm_lod, 1)
                last = split_mm(BB[0:40, :], (wm_hi[:, k, :], wm_lo[:, k, :]), (in_hi[:, k, :], in_lo[:, k, :]),
                                k == 0, k == KT - 1)
                if k == KT - 1:
                    last.then_inc(misc_sum, 1)

            group_steps(0, True, start_slot, misc_step)

            FOX_ADA = {11: 0, 20: 1, 31: 2}

            def fox_ada_slot(s, f):
                if s in FOX_ADA:
                    j = min(s // 3, 7)
                    pe.wait_ge(fsm, 8 * f + j + 1)
                    ada_columns(3 * f + (FOX_ADA[s] + Q_FOX), BA)

            def fox_slots(f):
                def slot(s):
                    if s - 1 in FOX_ADA:
                        pe.wait_ge(ada_col, 3 * f + (FOX_ADA[s - 1] + Q_FOX + 1))
                    fox_slot(s, f)
                    fox_ada_slot(s, f)
                return slot

            pe.wait_ge(cum_ready, 1)
            for t in range(TB):
                last = pe.transpose(BA[:, t * FOX_HEADS:(t + 1) * FOX_HEADS], f_z[32:40, t * P:t * P + P],
                                    ident[32:40, 32:40])
            last.then_inc(cumq_tr, 1)
            pe.wait_ge(cumq_ready, 1)
            with pe.Fori(1, FOX_GROUPS) as r:
                group_steps(r, False, fox_slots(r - 1))
            group_steps(FOX_GROUPS, False, fox_slots(FOX_GROUPS - 1))
            with pe.Fori(0, GLA_HEADS - 1) as h:
                group_steps(h + (FOX_GROUPS + 1), False, lambda s: gla_slot(s, h, h * 3 + Q_GLA))

            def out_steps(cg):
                for k in range(KT):
                    s, m = (k // 4) % 2, M_OUT + cg * MM_O + k // 4
                    hi, lo = wide_view(w_hi[s])[:, k % 4, :], wide_view(w_lo[s])[:, k % 4, :]
                    if k % 4 == 0:
                        pe.wait_ge(hi_done, m + 1)
                        pe.wait_ge(lo_done, m + 1)
                    if cg == 0:
                        pe.wait_ge(cat_lo, k + 1)
                    for t in range(TB):
                        if k == 0:
                            if cg == 0:
                                pe.wait_ge((ev_act, ev_dve)[t % 2], GROUPS * 3 - 2 + t // 2)
                            elif cg == 1:
                                pe.wait_ge(ev_act, GROUPS * 3)
                                pe.wait_ge(ev_dve, GROUPS * 3)
                                pe.wait_ge(gcat, 2 * GLA_HEADS)
                            else:
                                pe.wait_ge(y_mul, (cg - 2) * TB + t + 1)
                                if t == TB - 1:
                                    pe.wait_ge(ada_col, Q_GF - 3 + cg)
                        cols = slice(t * P, t * P + P)
                        last = split_mm(bank[4 * (cg % 2) + t][:, :], (in_hi[:, k, cols], in_lo[:, k, cols]), (hi, lo),
                                        k == 0, k == KT - 1)
                        if k == KT - 1 and t < TB - 1:
                            last.then_inc(y_sum, 1)
                        if t == TB - 1 and k % 4 == 3:
                            last.then_inc(w_used, 1)
                        if cg in (1, 2) and k == KT - 2 and t == 0:
                            pe.wait_ge(y_mul, cg * TB)
                            ada_rows(Q_GF - 3 + cg, bank[(3, 7)[cg - 1]])
                        if cg == 0 and t == 1:
                            gla_slot(2 * k, GLA_HEADS - 1, Q_GF - 3, True)
                    if cg == 0:
                        gla_slot(2 * k + 1, GLA_HEADS - 1, Q_GF - 3, True)

            for cg in range(CG):
                out_steps(cg)

            def x1_transpose(k):
                if k >= 4:
                    pe.wait_ge(mod_tmp, KT + k - 3)
                for t in range(TB):
                    last = pe.transpose(bank[4 + k % 4][:, t * P:t * P + P], y[:, t, k * P:k * P + P], ident[:, :])
                last.then_inc(x_tr, 1)

            pe.wait_ge(xn2_ready, 2)
            pe.wait_ge(xn2_dve, 2)
            pe.wait_ge(y_mul, CG * TB)
            for k in range(4):
                x1_transpose(k)

            def mlp_block(fb, first=False):
                for half in range(2):
                    for k in range(KT):
                        s, m = (k // 4) % 2, M_MLP + fb * MM_F + half * MM_O + k // 4
                        hi, lo = wide_view(w_hi[s])[:, k % 4, :], wide_view(w_lo[s])[:, k % 4, :]
                        if k % 4 == 0:
                            pe.wait_ge(hi_done, m + 1)
                            pe.wait_ge(lo_done, m + 1)
                        if first and half == 0:
                            pe.wait_ge(mod_lo, KT + k + 1)
                        for b in range(4):
                            if k == 0:
                                if half == 1:
                                    pe.wait_ge(h_relu, fb * FT + b + 1)
                            last = split_mm(bank[b][:, :], (hi[:, b * P:b * P + P], lo[:, b * P:b * P + P]),
                                            (in_hi[:, k, :], in_lo[:, k, :]), k == 0, k == KT - 1)
                            if k == KT - 1 and b < 3:
                                last.then_inc(h_sum, 1)
                            if half == 1 and k == KT - 2 and b == 0:
                                pe.wait_ge(y2_add, fb * 16 + 1)
                                ada_rows(fb + Q_GF, bank[7])
                        if k % 4 == 3:
                            last.then_inc(w_used, 1)
                        if first and half == 0 and k + 4 < KT:
                            x1_transpose(k + 4)
                for cg in range(CG):
                    for k in range(FT):
                        s, m = (k // 4) % 2, M_MLP + fb * MM_F + 2 * MM_O + cg * 2 + k // 4
                        hi, lo = wide_view(w_hi[s])[:, k % 4, :], wide_view(w_lo[s])[:, k % 4, :]
                        if k % 4 == 0:
                            pe.wait_ge(hi_done, m + 1)
                            pe.wait_ge(lo_done, m + 1)
                        if cg == 0:
                            pe.wait_ge(h_lo, fb * FT + k + 1)
                        for t in range(TB):
                            if k == 0:
                                if cg:
                                    pe.wait_ge(y2_add, fb * 16 + cg * 4 - 2 + t)
                                else:
                                    pe.wait_ge(y2_add, fb * 16 + 1)
                                if cg == 0 and t == 3:
                                    pe.wait_ge(ada_col, fb + Q_GF + 1)
                            cols = slice(t * P, t * P + P)
                            last = split_mm(bank[4 + t][:, :], (hid_hi[:, k, cols], hid_lo[:, k, cols]), (hi, lo),
                                            k == 0, k == FT - 1)
                            if k == FT - 1 and t < TB - 1:
                                last.then_inc(y2_sum, 1)
                        if k % 4 == 3:
                            last.then_inc(w_used, 1)

            mlp_block(0, first=True)
            with pe.Fori(1, FBS) as fb:
                mlp_block(fb)

        @block.scalar
        def _(act):
            def split_hi(m, arrived, n, view=slice(0, 2048)):
                act.wait_ge(w_in_s[n], arrived)
                act.wait_ge(w_used, m - 1)
                act.activation(w_hi[n][:, view], w_raw[n][:, view], ACT.Copy).then_inc(hi_done, 1)

            WIDE, NARROW = slice(0, 2048), slice(0, 2 * TILES * P)

            def next_hi_group(r, mm, last):
                if mm + 1 < MM_G or not last:
                    split_hi(r * MM_G + (mm + 1), arrived_group(r, mm + 1), (mm + 1) % 2, NARROW)

            def evict_group(r, scaled):
                for b in range(0, TILES, 2):
                    act.wait_ge(tile_sum, r * (TILES - 1) + b + 1)
                    act.activation(grp[:, b, :], bank[b][:, :], ACT.Copy,
                                   scale=FOX_DIM ** -0.5 if scaled and b == QA else 1.0).then_inc(ev_act, 1)

            def ada_times_c(q, half, b=0, arrived=None):
                if half == 0:
                    act.wait_ge(ada_in[b][0], 16 * (q - Q_FOX + KT // 2 + 1) if arrived is None else arrived)
                for k in range(half * KT // 2, (half + 1) * KT // 2):
                    last = act.activation((ada0, ada1)[b][0][:, k, :], (ada0, ada1)[b][0][:, k, :], ACT.Copy,
                                          scale=c_act[:, k:k + 1])
                if half:
                    last.then_inc(ada_mul[0], 1)

            ADA_TIMES = {5: (0, 0), 6: (0, 1), 14: (1, 0), 15: (1, 1), 24: (2, 0), 26: (2, 1)}

            def fox_tiles_free(f):
                act.wait_ge(fqk, 8 * f + 8)
                act.wait_ge(fvt, 2 * f + 2)

            def gla_tiles_free(h):
                act.wait_ge(go, 2 * h + 2)
                act.wait_ge(gkd, h + 1)
                act.wait_ge(gvt, 2 * h + 2)
                act.wait_ge(gcat, 2 * h + 2)

            def fox_slot(s, f):
                if s == 0:
                    act.wait_ge(cumb_in, 32 * (f + 1))
                    fox_bias(f, 0)
                if s == 1:
                    act.wait_ge(fvt, 2 * f + 1)
                    act.activation(fv_tok[:, 0, :, :], BB[:, :].rearrange("p (t d) -> p t d", t=TB), ACT.Copy)\
                        .then_inc(fvc, 1)
                    act.wait_ge(fvt, 2 * f + 2)
                    act.activation(fv_tok[:, 1, :, :], BA[:, :].rearrange("p (t d) -> p t d", t=TB), ACT.Copy)\
                        .then_inc(fvc, 1)
                if s % 3 == 1 and s // 3 < 8:
                    j = s // 3
                    n = (j % TB + 1) * P
                    act.wait_ge(fsm, 8 * f + j + 1)
                    if j:
                        act.wait_ge(fpt, 8 * f + j)
                    act.activation(prob[:, 0:n], logit[:, 0:n], ACT.Exp, bias=neg_max[:, j:j + 1],
                                   accum_out=row_sum[:, j:j + 1]).then_inc(fexp, 1)
                if s % 3 == 2 and s // 3 < 7:
                    fox_bias(f, s // 3 + 1)
                if s % 3 == 0 and 3 <= s <= 24:
                    j = s // 3 - 1
                    n = (j % TB + 1) * P
                    act.wait_ge(fpt, 8 * f + j + 1)
                    if j:
                        act.wait_ge(fpv, 9 * f + j)
                    act.activation(prob_t[:, 0:n], BB[:, 0:n], ACT.Copy).then_inc(fptc, 1)

            def fox_bias(f, j):
                i, head = j % TB, 2 * f + j // TB
                if j:
                    act.wait_ge(fsm, 8 * f + j)
                act.activation(bias[:, 0:(i + 1) * P], cumb[j // TB][:, 0:(i + 1) * P], ACT.Identity,
                               scale=-1.0, bias=cumq[:, i, bass.ds(head, 1)]).then_inc(fbr, 1)

            def gla_slot(s, h):
                if s == 2:
                    act.wait_ge(gaz, h + 1)
                    act.activation(g_e[:, :], g_e[:, :], ACT.Exp)
                    act.drain()
                    act.activation(g_e[:, :], g_e[:, :], ACT.Ln, bias=1.0).then_inc(gln, 1)
                if s in (2, 4):
                    half = s // 2 - 1
                    act.wait_ge(gvt, 2 * h + s // 2)
                    act.activation(gv_tok[:, :, half * P:half * P + P],
                                   BB[:, :].rearrange("p (t d) -> p t d", t=TB), ACT.Copy).then_inc(gvc, 1)
                if s == 5:
                    act.wait_ge(gdf, h + 1)
                    act.activation(g_dif[:, :, :], g_dif[:, :, :], ACT.Exp, scale=1.0 / GATE_TEMP)
                    act.activation(decay[:, :], g_cum[:, :, CHUNK - 1], ACT.Exp, scale=1.0 / GATE_TEMP)\
                        .then_inc(gde, 1)
                    act.activation(sig, grp[:, GR0:GR1 + 1, :], ACT.Exp, scale=-1.0).then_inc(gre, 1)
                if s == 8:
                    act.wait_ge(gkt, h + 1)
                    act.activation(kd_tok[:, :, :], BA[:, :].rearrange("p (t d) -> p t d", t=TB), ACT.Copy)\
                        .then_inc(gkc, 1)
                if s in (17, 18):
                    n = s - 17
                    act.wait_ge(go, 2 * h + n + 1)
                    act.activation(g_o[:, 2 * n:2 * n + 2, :],
                                   (BA, BB)[n][:, :].rearrange("p (t d) -> p t d", t=2), ACT.Copy,
                                   scale=GLA_DK ** -0.5).then_inc(goc, 1)

            act.wait_ge(c_tr, 1)
            act.activation(c_act[:, :], BB[:, 0:KT], ACT.Exp, scale=-1.0).then_inc(ce_ready, 1)
            act.wait_ge(c_ready, 1)

            def ada_m_times_c(q):
                ada_times_c(q, 0, q % 2, 16 * (q // 2 + 1))
                ada_times_c(q, 1, q % 2)

            ada_m_times_c(0)
            ada_m_times_c(1)
            for t in range(TB):
                act.wait_ge(x_in[t], 16)
                if t:
                    act.drain()
                act.activation(x_junk[:, :], x_raw[:, t, :], ACT.Square, accum_out=ss[:, t:t + 1]).then_inc(x_ss, 1)
            for k in range(0, KT, 2):
                act.wait_ge(x_tr, k + 1)
                act.activation(xn_t[:, k, :], bank[k % TILES][:, :], ACT.Copy).then_inc(xt_act, 1)
            act.wait_ge(x_tr, KT)
            act.wait_ge(xt_dve, KT // 2)

            def first_hi(m):
                act.wait_ge(w_in_s[m], arrived_group(0, m))
                act.activation(w_hi[m][:, NARROW], w_raw[m][:, NARROW], ACT.Copy).then_inc(hi_done, 1)

            def modulate(k):
                act.wait_ge(ada_col, k + 1)
                act.activation(in_tmp[:, k, :], xn_t[:, k, :], ACT.Identity, scale=mod_a[:, k:k + 1],
                               bias=mod_b[:, k:k + 1]).then_inc(mod_tmp, 1)
                act.wait_ge(mod_tmp, k + 1)
                act.activation(in_hi[:, k, :], in_tmp[:, k, :], ACT.Copy).then_inc(mod_hi, 1)

            act.wait_ge(wm_in, 32)
            act.activation(wm_hi[:, :, :], wm_raw[:, :, :], ACT.Copy).then_inc(wm_hid, 1)
            first_hi(0)
            modulate(0)
            for q in range(2, KT):
                ada_m_times_c(q)
                if q == 2:
                    first_hi(1)
                modulate(q - 1)
                if q % 2 == 0 and q >= 4:
                    split_hi(q // 2, arrived_group(0, q // 2), q // 2 % 2, NARROW)
            modulate(KT - 1)
            act.wait_ge(fz_abs, 1)
            act.activation(f_a[32:40, :], f_a[32:40, :], ACT.Exp)
            act.drain()
            act.activation(f_a[32:40, :], f_a[32:40, :], ACT.Ln, bias=1.0).then_inc(fz_ln, 1)
            split_hi(MM_G, arrived_group(1, 0), 0, NARROW)
            evict_group(0, True)
            act.wait_ge(cum_ready, 1)
            act.dma_start(cum_dram, f_z[32:40, :]).then_inc(cum_out, 16)
            act.wait_ge(cumq_tr, 1)
            act.activation(cumq[:, :, :], BA[:, 0:TB * FOX_HEADS].rearrange("p (t h) -> p t h", t=TB), ACT.Copy)\
                .then_inc(cumq_ready, 1)
            act.wait_ge(cumq_ready, 1)

            def cat_half(k):
                if k < 12:
                    act.wait_ge(w_used, (GROUPS - 1) * MM_G + k // 2 + 1)
                    if k == 0:
                        act.wait_ge(fob, 9 * FOX_GROUPS)
                    if k >= FOX_HEADS:
                        act.wait_ge(gcat, k + 1 - FOX_HEADS)
                act.activation(in_hi[:, k, :], cat[:, k, :], ACT.Copy).then_inc(cat_hi, 1)

            CAT_AT = {4 * (k // 2 + 1) + 2 + k % 2: k for k in range(12)}

            def group(r, work, q, last=False):
                for s in range(4 * MM_G):
                    work(s)
                    if last and s in CAT_AT:
                        cat_half(CAT_AT[s])
                    if s in ADA_TIMES:
                        ada_times_c(q + ADA_TIMES[s][0], ADA_TIMES[s][1])
                    if s % 4 == 0:
                        next_hi_group(r, s // 4, last)

            with act.Fori(1, FOX_GROUPS) as r:
                group(r, lambda s: fox_slot(s, r - 1), 3 * r + (Q_FOX - 3))
                fox_tiles_free(r - 1)
                evict_group(r, True)
            group(FOX_GROUPS, lambda s: fox_slot(s, FOX_GROUPS - 1), Q_GLA - 3)
            fox_tiles_free(FOX_GROUPS - 1)
            evict_group(FOX_GROUPS, False)
            def gla_group(h, last=False):
                group(h + (FOX_GROUPS + 1), lambda s: gla_slot(s, h), h * 3 + Q_GLA, last)
                if last:
                    split_hi(M_OUT, arrived_out(0, 0), 0)
                gla_tiles_free(h)
                evict_group(h + (FOX_GROUPS + 1), False)

            with act.Fori(0, GLA_HEADS - 2) as h:
                gla_group(h)
            gla_group(GLA_HEADS - 2, last=True)

            act.wait_ge(w_used, M_OUT)
            act.wait_ge(gcat, 2 * (GLA_HEADS - 1))
            for k in (KT - 4, KT - 3):
                cat_half(k)
            for s in range(2 * KT):
                gla_slot(s, GLA_HEADS - 1)
                if s in (5, 6):
                    ada_times_c(Q_GF - 3, s - 5)
                if s % 8 == 2 and s // 8 + 1 < MM_O:
                    split_hi(M_OUT + s // 8 + 1, arrived_out(0, s // 8 + 1), (s // 8 + 1) % 2)
                if s == 27:
                    for k in (KT - 2, KT - 1):
                        act.wait_ge(gcat, 2 * GLA_HEADS - KT + k + 1)
                        cat_half(k)

            def square_y(cg):
                for t in range(TB):
                    if t < TB - 1:
                        act.wait_ge(y_sum, cg * (TB - 1) + t + 1)
                    else:
                        act.wait_ge(w_used, M_OUT + cg * MM_O + MM_O)
                    act.activation(y[:, t, cg * 512:cg * 512 + 512], bank[4 * (cg % 2) + t][:, :], ACT.Square,
                                   accum_out=ss[:, t * CG + cg:t * CG + cg + 1]).then_inc(y_sq, 1)

            def split_hi_out(m):
                split_hi(M_OUT + m, RAW_OUT + 16 * (m // 2 + 1), m % 2)

            for cg in range(CG):
                if cg:
                    for mm in range(2, MM_O):
                        split_hi_out(cg * MM_O + mm)
                        if cg < 3:
                            ada_times_c(Q_GF - 3 + cg, mm - 2)
                split_hi_out(cg * MM_O + MM_O)
                square_y(cg)
                split_hi_out(cg * MM_O + MM_O + 1)

            act.wait_ge(y_rstd, 1)
            act.wait_ge(y_mul, CG * TB)
            act.activation(y[:, TB - 1, :], y[:, TB - 1, :], ACT.Copy, scale=rstd[:, TB - 1:TB]).then_inc(x1_part, 1)
            for t in range(TB - 1):
                act.wait_ge(x1_ready, t + 1)
                act.activation(y[:, t, :], x_res[:, t, :], ACT.Square, accum_out=ss[:, t:t + 1]).then_inc(x1_ss, 1)
            for t in (0, TB - 1):
                act.wait_ge(x1_rstd, 1 if t == 0 else 2)
                act.drain()
                act.activation(y[:, t, :], x_res[:, t, :], ACT.Copy, scale=rstd[:, 4 + t:5 + t]).then_inc(xn2_ready, 1)
                if t == 0:
                    for u in range(TB - 1):
                        act.dma_start(x1_t[:, u, :], x_res[:, u, :]).then_inc(x1_out, 16)
            act.dma_start(x1_t[:, TB - 1, :], x_res[:, TB - 1, :]).then_inc(x1_out, 16)
            for k in range(KT):
                act.wait_ge(mod_tmp, KT + k + 1)
                act.activation(in_hi[:, k, :], in_tmp[:, k, :], ACT.Copy).then_inc(mod_hi, 1)
                if k in (7, 11):
                    split_hi_out(CG * MM_O + k // 4 + 1)
            act.wait_ge(x1_out, 16 * TB)

            def hidden(fb, half):
                def relu(b):
                    if b < 3:
                        act.wait_ge(h_sum, fb * 6 + half * 3 + b + 1)
                    else:
                        act.wait_ge(w_used, M_MLP + fb * MM_F + half * MM_O + MM_O)
                    act.activation(hid_tmp[:, half * 4 + b, :], bank[b][:, :], ACT.Relu).then_inc(h_relu, 1)

                def hi(b):
                    act.wait_ge(h_sq, fb * FT + half * 4 + b + 1)
                    act.activation(hid_hi[:, half * 4 + b, :], hid_tmp[:, half * 4 + b, :], ACT.Copy).then_inc(h_hi, 1)

                act.wait_ge(w_used, M_MLP + fb * MM_F)
                for b in range(4):
                    relu(b)
                mm = (half + 1) * MM_O + 1
                split_hi(M_MLP + fb * MM_F + mm, arrived_mlp(fb, mm), mm % 2)
                for b in range(4):
                    hi(b)

            def square_y2(cg):
                act.drain()
                for t in range(TB):
                    act.wait_ge(y2_add, FBS * 16 - 14 + cg * TB + t)
                    act.activation(o_junk[:, t, :], y[:, t, cg * 512:cg * 512 + 512], ACT.Square,
                                   accum_out=ss[:, t * CG + cg:t * CG + cg + 1]).then_inc(o_sq, 1)

            def mlp_block(fb, first=False, last=False):
                for mm in range(MM_O if first else 0, MM_F):
                    if mm not in (MM_O + 1, 2 * MM_O + 1):
                        split_hi(M_MLP + fb * MM_F + mm, arrived_mlp(fb, mm), mm % 2)
                    if mm == MM_O:
                        hidden(fb, 0)
                    if mm in (MM_O + 1, MM_O + 2):
                        ada_times_c(fb + Q_GF, mm - MM_O - 1)
                    if mm == 2 * MM_O:
                        hidden(fb, 1)
                    if last and mm > 2 * MM_O and mm % 2 == 0:
                        square_y2((mm - 2 * MM_O) // 2 - 1)
                if last:
                    square_y2(CG - 1)

            mlp_block(0, first=True)
            with act.Fori(1, FBS - 1) as fb:
                mlp_block(fb)
            mlp_block(FBS - 1, last=True)
            act.wait_ge(o_rstd, 1)
            act.wait_ge(o_mul, CG - 1)
            act.wait_ge(o_mul_last, TB)
            act.activation(y[:, TB - 1, :], y[:, TB - 1, :], ACT.Copy, scale=rstd[:, TB - 1:TB]).then_inc(o_part, 1)

        @block.vector
        def _(dve):
            def split_lo(m, n, view=slice(0, 2048)):
                dve.wait_ge(hi_done, m + 1)
                dve.wait_ge(w_used, m - 1)
                dve.tensor_tensor(w_lo[n][:, view], w_raw[n][:, view], w_hi[n][:, view].bitcast(F32), ALU.subtract)\
                    .then_inc(lo_done, 1)

            NARROW = slice(0, 2 * TILES * P)

            def evict_group(r, scaled):
                for b in range(1, TILES, 2):
                    if b < TILES - 1:
                        dve.wait_ge(tile_sum, r * (TILES - 1) + b + 1)
                    else:
                        dve.wait_ge(w_used, r * MM_G + MM_G)
                    if scaled and b == QB:
                        dve.tensor_scalar(grp[:, b, :], bank[b][:, :], FOX_DIM ** -0.5, None, ALU.mult)\
                            .then_inc(ev_dve, 1)
                    else:
                        dve.tensor_copy(grp[:, b, :], bank[b][:, :]).then_inc(ev_dve, 1)

            def fox_tiles_free(f):
                dve.wait_ge(fqk, 8 * f + 8)
                dve.wait_ge(fvt, 2 * f + 2)

            def gla_tiles_free(h):
                dve.drain()
                dve.wait_ge(go, 2 * h + 2)
                dve.wait_ge(gvt, 2 * h + 2)
                dve.wait_ge(gre, h + 1)

            def ada_reduce(q, u, b=0, used=None):
                if u == 0:
                    dve.wait_ge(ada_sum, q if used is None else used)
                dve.wait_ge(ada_mul[u], q + 1)
                dve.tensor_reduce(acc[b][:, u * P:(u + 1) * P], (ada0, ada1)[b][u][:, :, :].rearrange("p k n -> p n k"),
                                  AX_X, ALU.add).then_inc(ada_acc[u], 1)

            def mod_columns(q, k, dst, c_scale, c_shift, c_gain):
                dve.wait_ge(ada_sum, q + 1)
                dve.tensor_scalar(mod_a[:, bass.ds(k, 1)], dst[:, 0:1], cols_a[:, bass.ds(k + c_scale, 1)],
                                  cols_a[:, bass.ds(k + c_gain, 1)], ALU.add, ALU.mult)
                dve.tensor_tensor(mod_b[:, bass.ds(k, 1)], dst[:, 1:2], cols_a[:, bass.ds(k + c_shift, 1)], ALU.add)\
                    .then_inc(ada_col, 1)

            def gate_row(q, k, src, k0=0):
                dve.wait_ge(bg_in, 32 * (k + k0 + 1))
                dve.wait_ge(ada_sum, q + 1)
                part = gg[:, bass.ds(k * 2 * P, 2 * P)]
                dve.tensor_tensor(part, src[:, 0:2 * P], bg_bc[:, 0, :], ALU.add)
                dve.drain()
                dve.tensor_tensor(part, part, bg_bc[:, 1, :], ALU.mult).then_inc(ada_col, 1)

            ADA_SUM = {7: (0, 0), 10: (0, 1), 16: (1, 0), 19: (1, 1), 27: (2, 0), 30: (2, 1)}
            ADA_SUM_GLA = {7: (0, 0), 8: (0, 1), 16: (1, 0), 17: (1, 1), 28: (2, 0), 29: (2, 1)}
            F_COL = {11: 0, 20: 1, 31: 2}

            def fox_slot(s, f):
                if s % 3 == 0 and s // 3 < 8:
                    j = s // 3
                    n = (j % TB + 1) * P
                    diag = slice(n - P, n)
                    if j:
                        dve.wait_ge(fexp, 8 * f + j)
                    dve.wait_ge(fbr, 8 * f + j + 1)
                    dve.wait_ge(fqk, 8 * f + j + 1)
                    dve.tensor_tensor(bias[:, diag], bias[:, diag], causal[:, :], ALU.min)
                    dve.drain()
                    dve.tensor_tensor_reduce(logit[:, 0:n], BA[:, 0:n], bias[:, 0:n], 1.0, MASKED,
                                             ALU.add, ALU.max, row_max[:, j:j + 1])
                    dve.drain()
                    dve.tensor_scalar(neg_max[:, j:j + 1], row_max[:, j:j + 1], -1.0, None, ALU.mult)\
                        .then_inc(fsm, 1)
                if s in F_COL:
                    k = 3 * f + F_COL[s]
                    mod_columns(k + Q_FOX, k, BA, C_SCF, C_SHF, C_GPRE2)
                if s % 3 == 1 and 4 <= s <= 25:
                    j = (s - 4) // 3
                    dve.wait_ge(fexp, 8 * f + j + 1)
                    dve.reciprocal(row_inv[:, j:j + 1], row_sum[:, j:j + 1])
                    dve.drain()
                    dve.wait_ge(fpv, 9 * f + j + 1)
                    if j:
                        fox_store(f, j - 1)
                    dve.tensor_scalar(f_o[:, :], BB[:, 0:P], row_inv[:, j:j + 1], None, ALU.mult).then_inc(fob, 1)
                    dve.drain()
                    dve.tensor_tensor_reduce(f_junk[:, :], f_o[:, :], f_o[:, :], 1.0 / FOX_DIM, EPS, ALU.mult, ALU.add,
                                             f_ms[:, j:j + 1]).then_inc(fss, 1)
                if s % 3 == 0 and 6 <= s <= 27:
                    j = s // 3 - 2
                    dve.wait_ge(frn, 8 * f + j + 1)
                    dve.tensor_scalar(f_o[:, :], f_o[:, :], f_r[:, j:j + 1], None, ALU.mult).then_inc(fon, 1)
                if s == 28:
                    dve.wait_ge(fpv, 9 * f + 9)
                    fox_store(f, 7).then_inc(fob, 1)
                    dve.drain()

            def fox_store(f, j):
                i, head = j % TB, 2 * f + j // TB
                return dve.tensor_scalar(cat[:, bass.ds(head, 1), i * P:i * P + P].rearrange("p o n -> p (o n)"),
                                         BB[:, P:2 * P], cols_b[:, bass.ds(head + B_GFOX, 1)], None, ALU.mult)

            SIG_AT, SIG_MUL = (14, 21), 22

            def gla_slot(s, h, ada, last_head=False):
                if s == 0:
                    dve.drain()
                    dve.wait_ge(gz, h + 1)
                    dve.tensor_scalar(g_z[:, :], BA[:, :], cols_b[:, bass.ds(h + B_A2, 1)], None, ALU.add)
                    dve.drain()
                    dve.scalar_tensor_tensor(g_e[:, :], g_z[:, :], -1.0, g_z[:, :], ALU.mult, ALU.min).then_inc(gaz, 1)
                if s == 3:
                    dve.wait_ge(gln, h + 1)
                    dve.scalar_tensor_tensor(g_z[:, :], g_z[:, :], 0.0, g_e[:, :], ALU.min, ALU.subtract)
                    dve.drain()
                    dve.tensor_tensor_scan(g_cum[:, :, :].rearrange("p n c -> p (n c)"), chunk_on[:, :], g_z[:, :],
                                           0.0, ALU.mult, ALU.add)
                    dve.drain()
                    dve.tensor_tensor(g_dif[:, :, :], g_cum[:, :, CHUNK - 1:CHUNK].to_broadcast([P, NCH, CHUNK]),
                                      g_cum[:, :, :], ALU.subtract).then_inc(gdf, 1)
                if s == 6:
                    dve.wait_ge(gde, h + 1)
                    dve.tensor_tensor(g_e[:, :], grp[:, GK, :], g_dif[:, :, :].rearrange("p n c -> p (n c)"),
                                      ALU.mult).then_inc(gkd, 1)
                if s == 7:
                    dve.wait_ge(gre, h + 1)
                    dve.tensor_scalar(sig, sig, 1.0, None, ALU.add)
                if s in SIG_AT:
                    dve.drain()
                    dve.reciprocal(sig[:, SIG_AT.index(s), :], sig[:, SIG_AT.index(s), :])
                if s == SIG_MUL:
                    dve.drain()
                    dve.tensor_tensor(sig, sig, grp[:, GR0:GR1 + 1, :], ALU.mult)
                if s == 12:
                    mod_columns(ada, h + 3 * FOX_GROUPS, BB, C_SCF, C_SHF, C_GPRE2)
                if s in (10, 13):
                    n0 = 4 * (s == 13)
                    dve.wait_ge(gu, 2 * h + 1 + (s == 13))
                    for n in range(n0, n0 + 4):
                        u = (BA, BB)[n % 2][:, (n - n0) // 2 * GLA_DV:((n - n0) // 2 + 1) * GLA_DV]
                        if n == 0:
                            last = dve.tensor_copy(states[:, 0, :], u)
                        else:
                            last = dve.scalar_tensor_tensor(states[:, n, :], states[:, n - 1, :],
                                                            decay[:, n:n + 1], u, ALU.mult, ALU.add)
                        if n % 4 < 3:
                            dve.drain()
                    last.then_inc(gst, 1)
                    dve.drain()
                if s == 18:
                    dve.wait_ge(goc, 2 * h + 2)
                    for t in range(TB):
                        last = dve.tensor_tensor_reduce(g_junk[:, :], g_o[:, t, :], g_o[:, t, :], 1.0 / GLA_DV, EPS,
                                                        ALU.mult, ALU.add, ms[:, t:t + 1])
                        if t < TB - 1:
                            dve.drain()
                    last.then_inc(gss, 1)
                if s == 20:
                    dve.wait_ge(grn, h + 1)
                    for t in range(TB):
                        last = dve.tensor_scalar(g_o[:, t, :], g_o[:, t, :], rstd[:, t:t + 1], None, ALU.mult)
                    last.then_inc(gon, 1)
                    if not last_head:
                        gate_row(ada + 1, h * 2, BA)
                if s in (24, 25):
                    half = s - 24
                    dve.drain()
                    dve.wait_ge(gt, 2 * h + half + 1)
                    row = cat[:, bass.ds(h * 2 + (FOX_HEADS + half), 1), :].rearrange("p o n -> p (o n)")
                    dve.scalar_tensor_tensor(row, (BA, BB)[half][:, :], cols_b[:, bass.ds(h * 2 + (B_GGLA + half), 1)],
                                             sig[:, half, :], ALU.mult, ALU.mult).then_inc(gcat, 1)
                if s == 31 and not last_head:
                    gate_row(ada + 2, h * 2 + 1, BA)

            dve.wait_ge(ce_ready, 1)
            dve.tensor_scalar(c_act[:, :], c_act[:, :], 1.0, None, ALU.add)
            dve.drain()
            dve.reciprocal(c_act[:, :], c_act[:, :])
            dve.drain()
            dve.tensor_tensor(c_act[:, :], c_act[:, :], BB[:, 0:KT], ALU.mult).then_inc(c_ready, 1)
            for q in range(2):
                ada_reduce(q, 0, q, 0)
                ada_reduce(q, 1, q)
            dve.wait_ge(rows_tr, 1)
            dve.tensor_copy(cols_a[:, :], BA[:, 0:6 * KT])
            dve.tensor_copy(cols_b[:, :], BA[:, 128:148])
            dve.drain()
            for col in (C_SCM, C_SCF):
                last = dve.tensor_scalar(cols_a[:, col:col + KT], cols_a[:, col:col + KT], 1.0, None, ALU.add)
            last.then_inc(cols_ready, 1)
            for t in range(TB):
                dve.wait_ge(x_rstd, t + 1)
                dve.tensor_scalar(x_raw[:, t, :], x_raw[:, t, :], rstd[:, t:t + 1], None, ALU.mult)\
                    .then_inc(xn_ready, 1)
            for k in range(1, KT, 2):
                dve.wait_ge(x_tr, k + 1)
                dve.tensor_copy(xn_t[:, k, :], bank[k % TILES][:, :]).then_inc(xt_dve, 1)

            def modulated_lo(k, n):
                dve.wait_ge(mod_hi, n + 1)
                dve.tensor_tensor(in_lo[:, k, :], in_tmp[:, k, :], in_hi[:, k, :].bitcast(F32), ALU.subtract).then_inc(mod_lo, 1)

            def first_lo(m):
                dve.wait_ge(hi_done, m + 1)
                dve.tensor_tensor(w_lo[m][:, NARROW], w_raw[m][:, NARROW], w_hi[m][:, NARROW].bitcast(F32),
                                  ALU.subtract).then_inc(lo_done, 1)

            def mod_columns_m(q):
                mod_columns(q, q, BA[:, 0:2], C_SCM, C_SHM, C_GPRE)

            mod_columns_m(0)
            dve.wait_ge(wm_hid, 1)
            dve.tensor_tensor(wm_lo[:, :, :], wm_raw[:, :, :], wm_hi[:, :, :].bitcast(F32), ALU.subtract)\
                .then_inc(wm_lod, 1)
            mod_columns_m(1)
            first_lo(0)
            modulated_lo(0, 0)
            for q in range(2, KT):
                ada_reduce(q, 0, q % 2, q - 1)
                ada_reduce(q, 1, q % 2)
                mod_columns_m(q)
                if q == 2:
                    first_lo(1)
                modulated_lo(q - 1, q - 1)
                if q % 2 == 0 and q >= 4:
                    split_lo(q // 2, q // 2 % 2, NARROW)
            modulated_lo(KT - 1, KT - 1)
            dve.wait_ge(misc_sum, 1)
            dve.wait_ge(bfg_in, 16)
            dve.tensor_scalar(f_z[32:40, :], BB[32:40, :], b_fg[32:40, 0:1], None, ALU.add)
            dve.tensor_copy(ga_t[:, :], BB[0:RANK, :]).then_inc(ga_ready, 1)
            dve.drain()
            dve.scalar_tensor_tensor(f_a[32:40, :], f_z[32:40, :], -1.0, f_z[32:40, :], ALU.mult, ALU.min)\
                .then_inc(fz_abs, 1)
            dve.wait_ge(fz_ln, 1)
            dve.scalar_tensor_tensor(f_a[32:40, :], f_z[32:40, :], 0.0, f_a[32:40, :], ALU.min, ALU.subtract)
            dve.drain()
            dve.wait_ge(consts, 2)
            dve.tensor_tensor_scan(f_z[32:40, :], ones[32:40, 0:1].to_broadcast([8, SEQ]), f_a[32:40, :], 0.0,
                                   ALU.mult, ALU.add).then_inc(cum_ready, 1)
            split_lo(MM_G, 0, NARROW)
            evict_group(0, True)

            def cat_half(k):
                dve.wait_ge(cat_hi, k + 1)
                dve.tensor_tensor(in_lo[:, k, :], cat[:, k, :], in_hi[:, k, :].bitcast(F32), ALU.subtract).then_inc(cat_lo, 1)

            CAT_AT = {4 * (k // 2 + 1) + 2 + k % 2: k for k in range(12)}

            def group(r, work, q, ada_sum, last=False):
                for s in range(4 * MM_G):
                    work(s)
                    if last and s in CAT_AT:
                        cat_half(CAT_AT[s])
                    if s in ada_sum:
                        ada_reduce(q + ada_sum[s][0], ada_sum[s][1])
                    if s % 4 == 0 and (s // 4 + 1 < MM_G or not last):
                        split_lo(r * MM_G + (s // 4 + 1), (s // 4 + 1) % 2, NARROW)

            with dve.Fori(1, FOX_GROUPS) as r:
                group(r, lambda s: fox_slot(s, r - 1), 3 * r + (Q_FOX - 3), ADA_SUM)
                fox_tiles_free(r - 1)
                evict_group(r, True)
            group(FOX_GROUPS, lambda s: fox_slot(s, FOX_GROUPS - 1), Q_GLA - 3, ADA_SUM)
            fox_tiles_free(FOX_GROUPS - 1)
            evict_group(FOX_GROUPS, False)
            def gla_group(h, last=False):
                group(h + (FOX_GROUPS + 1), lambda s: gla_slot(s, h, h * 3 + Q_GLA), h * 3 + Q_GLA, ADA_SUM_GLA, last)
                if last:
                    split_lo(M_OUT, 0)
                gla_tiles_free(h)
                evict_group(h + (FOX_GROUPS + 1), False)

            with dve.Fori(0, GLA_HEADS - 2) as h:
                gla_group(h)
            gla_group(GLA_HEADS - 2, last=True)

            for k in (KT - 4, KT - 3):
                cat_half(k)
            for s in range(2 * KT):
                gla_slot(s, GLA_HEADS - 1, Q_GF - 3, True)
                if s in (7, 8):
                    ada_reduce(Q_GF - 3, s - 7)
                if s % 8 == 2 and s // 8 + 1 < MM_O:
                    split_lo(M_OUT + s // 8 + 1, (s // 8 + 1) % 2)
                if s == 27:
                    cat_half(KT - 2)
                    cat_half(KT - 1)

            def gain_y(cg):
                for t in range(TB):
                    if cg == CG - 1 and t == TB - 1:
                        dve.wait_ge(y_sq, CG * TB)
                        dve.tensor_reduce(ss4[:, :], ss[:, :].rearrange("p (t g) -> p t g", g=CG), AX_X, ALU.add)\
                            .then_inc(y_gate, 1)
                    dve.wait_ge(y_sq, cg * TB + t + 1)
                    cols = slice(cg * 512, cg * 512 + 512)
                    dve.tensor_tensor(y[:, t, cols], bank[4 * (cg % 2) + t][:, :], gg[:, cols], ALU.mult)\
                        .then_inc(y_mul, 1)

            for cg in range(CG):
                if cg:
                    for mm in range(2, MM_O):
                        split_lo(M_OUT + cg * MM_O + mm, mm % 2)
                    if cg < 3:
                        ada_reduce(Q_GF - 3 + cg, 0)
                        ada_reduce(Q_GF - 3 + cg, 1)
                        gate_row(Q_GF - 3 + cg, KT // 2 - 3 + cg, bank[(3, 7)[cg - 1]])
                        dve.drain()
                split_lo(M_OUT + cg * MM_O + MM_O, 0)
                gain_y(cg)
                if cg < CG - 1:
                    split_lo(M_OUT + cg * MM_O + MM_O + 1, 1)
            dve.drain()
            dve.wait_ge(y_rstd, 1)
            for t in range(TB - 1):
                dve.wait_ge(xres_in[t], 16)
                dve.scalar_tensor_tensor(x_res[:, t, :], y[:, t, :], rstd[:, t:t + 1], x_res[:, t, :], ALU.mult,
                                         ALU.add).then_inc(x1_ready, 1)
            dve.wait_ge(x1_pool, 1)
            dve.tensor_tensor_reduce(y[:, TB - 1, :], x_res[:, TB - 1, :], x_res[:, TB - 1, :], 1.0, 0.0,
                                     ALU.mult, ALU.add, ss[:, TB - 1:TB]).then_inc(x1_sq, 1)
            for t in range(1, TB - 1):
                dve.wait_ge(x1_rstd, 1 if t == 1 else 2)
                dve.tensor_scalar(y[:, t, :], x_res[:, t, :], rstd[:, 4 + t:5 + t], None, ALU.mult).then_inc(xn2_dve, 1)
            for k in range(KT):
                dve.wait_ge(x_tr, KT + k + 1)
                dve.tensor_scalar(in_tmp[:, k, :], bank[4 + k % 4][:, :], mod_a[:, k:k + 1], mod_b[:, k:k + 1],
                                  ALU.mult, ALU.add).then_inc(mod_tmp, 1)
                if k:
                    modulated_lo(k - 1, KT + k - 1)
                if k in (2, 8, 12):
                    split_lo(M_MLP + max(k // 4, 1), max(k // 4, 1) % 2)
            modulated_lo(KT - 1, 2 * KT - 1)
            dve.memset(y[:, :, :], 0.0).then_inc(y2_add, 1)
            dve.drain()

            def hidden(fb, half):
                def square(b):
                    dve.wait_ge(h_relu, fb * FT + half * 4 + b + 1)
                    dve.tensor_tensor(hid_tmp[:, half * 4 + b, :], hid_tmp[:, half * 4 + b, :],
                                      hid_tmp[:, half * 4 + b, :], ALU.mult).then_inc(h_sq, 1)

                def lo(b):
                    dve.wait_ge(h_hi, fb * FT + half * 4 + b + 1)
                    dve.tensor_tensor(hid_lo[:, half * 4 + b, :], hid_tmp[:, half * 4 + b, :],
                                      hid_hi[:, half * 4 + b, :].bitcast(F32), ALU.subtract).then_inc(h_lo, 1)

                for b in range(4):
                    square(b)
                mm = (half + 1) * MM_O + 1
                split_lo(M_MLP + fb * MM_F + mm, mm % 2)
                for b in range(4):
                    lo(b)

            def add_y2(fb, cg):
                for t in range(TB):
                    if t < TB - 1:
                        dve.wait_ge(y2_sum, (fb * CG + cg) * (TB - 1) + t + 1)
                    else:
                        dve.wait_ge(w_used, M_MLP + fb * MM_F + 2 * MM_O + cg * 2 + 2)
                    part = y[:, t, cg * 512:cg * 512 + 512]
                    dve.tensor_tensor(part, bank[4 + t][:, :], part, ALU.add).then_inc(y2_add, 1)

            def mlp_block(fb, first=False, last=False):
                for mm in range(MM_O if first else 1, MM_F):
                    if mm not in (MM_O + 1, 2 * MM_O + 1):
                        split_lo(M_MLP + fb * MM_F + mm, mm % 2)
                    if mm == MM_O:
                        hidden(fb, 0)
                    if mm == MM_O + 3:
                        ada_reduce(fb + Q_GF, 0)
                        ada_reduce(fb + Q_GF, 1)
                    if mm == 2 * MM_O - 1:
                        gate_row(fb + Q_GF, fb, bank[7], KT // 2)
                    if mm == 2 * MM_O:
                        hidden(fb, 1)
                    if mm > 2 * MM_O and mm % 2 == 0:
                        add_y2(fb, (mm - 2 * MM_O) // 2 - 1)
                if not last:
                    split_lo(M_MLP + fb * MM_F + MM_F, 0)
                add_y2(fb, CG - 1)

            mlp_block(0, first=True)
            with dve.Fori(1, FBS - 1) as fb:
                mlp_block(fb)
            mlp_block(FBS - 1, last=True)
            dve.wait_ge(o_sq, CG * TB)
            dve.tensor_reduce(ss4[:, :], ss[:, :].rearrange("p (t g) -> p t g", g=CG), AX_X, ALU.add).then_inc(o_ss, 1)
            dve.drain()
            for t in range(TB):
                cols = slice((CG - 1) * 512, CG * 512)
                dve.tensor_tensor(y[:, t, cols], y[:, t, cols], gg[:, cols], ALU.mult).then_inc(o_mul_last, 1)
            dve.drain()
            dve.wait_ge(o_mul, CG - 1)
            dve.wait_ge(o_rstd, 1)
            for t in range(TB - 1):
                dve.wait_ge(x1_in[t], 16)
                dve.scalar_tensor_tensor(x1_end[:, t, :], y[:, t, :], rstd[:, t:t + 1], x1_end[:, t, :], ALU.mult,
                                         ALU.add).then_inc(o_ready, 1)

        @block.gpsimd
        def _(pool):
            def inverse_root(dst, mean, total, n):
                pool.tensor_scalar(mean, total, 1.0 / n, EPS, ALU.mult, ALU.add)
                pool.drain()
                return pool.tensor_tensor(dst, mean, neg_half[:, 0:mean.shape[1]], ALU.pow)

            def ada_second(q, b=0, arrived=None):
                pool.wait_ge(ada_in[b][1], 16 * (q - Q_FOX + KT // 2 + 1) if arrived is None else arrived)
                unit = (ada0, ada1)[b][1]
                pool.tensor_tensor(unit[:, :, :], unit[:, :, :],
                                   c_act[:, :].rearrange("p (k o) -> p k o", o=1).to_broadcast([P, KT, P]), ALU.mult)\
                    .then_inc(ada_mul[1], 1)

            pool.memset(ident[:, :], 0.0)
            pool.memset(ones[:, :], 1.0)
            pool.drain()
            pool.affine_select(out=ident[:, :], in_=ident[:, :], compare_op=ALU.not_equal, fill=1.0,
                               base=0, pattern=[[-1, P]], channel_multiplier=1).then_inc(consts, 1)
            pool.memset(wm_raw[:, :, :], 0.0).then_inc(wm_zero, 1)
            pool.memset(neg_half[:, :], -0.5)
            pool.memset(causal[:, :], -MASKED)
            pool.memset(chunk_on[:, :], 1.0)
            pool.drain()
            pool.affine_select(out=causal[:, :], in_=causal[:, :], compare_op=ALU.is_ge, fill=MASKED,
                               base=0, pattern=[[-1, P]], channel_multiplier=1)
            pool.memset(chunk_on[:, :].rearrange("p (n c) -> p n c", c=CHUNK)[:, :, 0:1], 0.0).then_inc(consts, 1)
            pool.wait_ge(c_ready, 1)
            ada_second(0, 0, 16)
            ada_second(1, 1, 16)
            for t in range(TB):
                pool.wait_ge(x_ss, t + 1)
                inverse_root(rstd[:, t:t + 1], ms[:, t:t + 1], ss[:, t:t + 1], D).then_inc(x_rstd, 1)
            for q in range(2, KT):
                ada_second(q, q % 2, 16 * (q // 2 + 1))

            def fox(f):
                MUL = {5: 0, 14: 1, 23: 2}
                for s in range(32):
                    if s % 3 == 1 and 4 <= s <= 25:
                        j = (s - 4) // 3
                        pool.wait_ge(fss, 8 * f + j + 1)
                        pool.tensor_tensor(f_r[:, j:j + 1], f_ms[:, j:j + 1], neg_half[:, 0:1], ALU.pow)\
                            .then_inc(frn, 1)
                    if s in MUL:
                        ada_second(3 * f + (MUL[s] + Q_FOX))

            def gla(h, q, last_head=False):
                ada_second(q)
                if not last_head:
                    ada_second(q + 1)
                pool.wait_ge(gss, h + 1)
                pool.tensor_tensor(rstd[:, 0:TB], ms[:, 0:TB], neg_half[:, 0:TB], ALU.pow).then_inc(grn, 1)
                if not last_head:
                    ada_second(q + 2)

            with pool.Fori(0, FOX_GROUPS - 1) as f:
                fox(f)
            fox(FOX_GROUPS - 1)
            with pool.Fori(0, GLA_HEADS - 1) as h:
                gla(h, h * 3 + Q_GLA)
            gla(GLA_HEADS - 1, Q_GF - 3, True)
            ada_second(Q_GF - 2)
            ada_second(Q_GF - 1)
            pool.wait_ge(y_gate, 1)
            inverse_root(rstd[:, 0:TB], ms[:, 0:TB], ss4[:, :], D).then_inc(y_rstd, 1)
            pool.wait_ge(xres_in[TB - 1], 16)
            pool.wait_ge(x1_part, 1)
            pool.tensor_tensor(x_res[:, TB - 1, :], x_res[:, TB - 1, :], y[:, TB - 1, :], ALU.add).then_inc(x1_pool, 1)
            for n in range(2):
                pool.wait_ge(x1_ss, 2 + n)
                if n:
                    pool.wait_ge(x1_sq, 1)
                two = slice(2 * n, 2 * n + 2)
                inverse_root(rstd[:, 4 + 2 * n:6 + 2 * n], ms[:, two], ss[:, two], D).then_inc(x1_rstd, 1)
            with pool.Fori(0, FBS) as fb:
                ada_second(fb + Q_GF)
            pool.wait_ge(ada_col, Q_GF + FBS)
            for cg in range(CG - 1):
                pool.wait_ge(o_sq, cg * TB + TB)
                cols = slice(cg * 512, cg * 512 + 512)
                pool.tensor_tensor(y[:, :, cols], y[:, :, cols],
                                   gg[:, cols].rearrange("p (o n) -> p o n", o=1).to_broadcast([P, TB, 512]),
                                   ALU.mult).then_inc(o_mul, 1)
            pool.wait_ge(o_ss, 1)
            inverse_root(rstd[:, 0:TB], ms[:, 0:TB], ss4[:, :], D).then_inc(o_rstd, 1)
            pool.wait_ge(x1_in[TB - 1], 16)
            pool.wait_ge(o_part, 1)
            pool.tensor_tensor(x1_end[:, TB - 1, :], x1_end[:, TB - 1, :], y[:, TB - 1, :], ALU.add).then_inc(o_pool, 1)


_INS = ["x", "c", "w_ada", "b_ada", "g_pre_mix", "g_post_mix", "w_in", "b_fgate", "w_gla_a2", "b_gla_a2",
        "g_fox_out", "g_gla_out", "w_out", "g_pre_mlp", "g_post_mlp", "w_mlp_in", "w_mlp_out"]


def kernel(**inputs):
    import concourse.bacc as bacc
    from concourse.bass_utils import run_bass_kernel_spmd

    nc = bacc.Bacc("TRN2", target_bir_lowering=False, num_devices=1)
    arrays, args = {}, []
    for name in _INS:
        a = np.ascontiguousarray(inputs[name])
        arrays[f"in_{name}"] = a
        args.append(nc.dram_tensor(f"in_{name}", a.shape, mybir.dt.from_np(a.dtype), kind="ExternalInput").ap())
    shape = inputs["x"].shape
    args.append(nc.dram_tensor("out", shape, F32, kind="ExternalOutput").ap())
    build_block(nc, *args)
    r = run_bass_kernel_spmd(nc, [arrays], core_ids=[0])
    return r.results[0]["out"]
```

```python
from contextlib import ExitStack

import numpy as np

import concourse.bass as bass
from concourse import mybir

F32 = mybir.dt.float32
F32R = mybir.dt.float32r
ALU = mybir.AluOpType
ACT = mybir.ActivationFunctionType
AX_X = mybir.AxisListType.X

P = 128
KIB = 1024


def build_block(nc, x, c, w_ada, b_ada, g_pre_mix, g_post_mix, w_in, b_fgate, w_gla_a2, b_gla_a2,
                g_fox_out, g_gla_out, w_out, g_pre_mlp, g_post_mlp, w_mlp_in, w_mlp_out, out):
    _, SEQ, D = x.shape
    KT = D // P
    TB = SEQ // P
    FOX_HEADS, FOX_DIM = g_fox_out.shape[1:]
    GLA_HEADS, GLA_DV = g_gla_out.shape[1:]
    RANK, GLA_KEYS = w_gla_a2.shape[1:]
    GLA_DK = GLA_KEYS // GLA_HEADS
    FOX_WIDTH = FOX_HEADS * FOX_DIM
    GLA_WIDTH = GLA_HEADS * GLA_DV
    D_FF = w_mlp_in.shape[2]
    CHUNK = 64
    NCH = SEQ // CHUNK
    EPS = 1e-6
    GATE_TEMP = 16.0
    MASKED = float(np.finfo(np.float32).min)
    assert FOX_DIM == P and GLA_DK == P and GLA_DV == 2 * P and SEQ == 512 and KT == 16

    FF_COL = 3 * FOX_WIDTH
    GQ_COL = FF_COL + FOX_HEADS
    GK_COL = GQ_COL + GLA_KEYS
    GV_COL = GK_COL + GLA_KEYS
    GA_COL = GV_COL + GLA_WIDTH
    GR_COL = GA_COL + RANK

    TILES = 6
    FOX_GROUPS = FOX_HEADS // 2
    GROUPS = FOX_GROUPS + GLA_HEADS
    QA, QB, KA, KB, VA, VB = range(6)
    GQ, GK, GV0, GV1, GR0, GR1 = range(6)
    MM_G = KT // 2
    MM_O = KT // 4
    CG = D // 512
    FBLK = 1024
    FT = FBLK // P
    FBS = D_FF // FBLK
    M_OUT = GROUPS * MM_G
    M_MLP = M_OUT + CG * MM_O
    MM_F = 2 * MM_O + CG * 2
    GROUP_DMAS = 4
    RAW_OUT = 16 * GROUP_DMAS * (GROUPS * MM_G // 2)
    RAW_MLP = RAW_OUT + 16 * (CG * MM_O // 2)

    SHIFT_M, SCALE_M, GATE_M, SHIFT_F, SCALE_F, GATE_F = [n * D for n in range(6)]
    Q_FOX = KT
    Q_GLA = Q_FOX + 3 * FOX_GROUPS
    Q_GF = Q_GLA + 3 * GLA_HEADS

    x_t = x[0].rearrange("(t p) d -> p t d", p=P)
    out_t = out[0].rearrange("(t p) d -> p t d", p=P)
    w_ada_t = w_ada[0].rearrange("(k p) n -> p k n", p=P)
    w_in_t = w_in[0].rearrange("(k p) n -> p k n", p=P)
    w_out_t = w_out[0].rearrange("(k p) n -> p k n", p=P)
    w_m1_t = w_mlp_in[0].rearrange("(k p) n -> p k n", p=P)
    w_m2_t = w_mlp_out[0].rearrange("(k p) n -> p k n", p=P)

    with ExitStack() as ctx:
        base = 16512
        R_A = base
        R_B = R_A + 64 * KIB
        R_C = R_B + 32 * KIB
        R_G = R_C + 48 * KIB
        R_T = R_G + 12 * KIB
        R_AD = R_G + 32 * KIB
        R_GG = R_AD + 16 * KIB
        R_K = R_GG + 8 * KIB

        def at(name, shape, offset, dt=F32):
            return nc.alloc_sbuf_tensor_at(name, shape, dt, offset=offset)

        in_hi = at("in_hi", [P, KT, SEQ], R_A, F32R)
        in_lo = at("in_lo", [P, KT, SEQ], R_A + 32 * KIB, F32R)
        in_tmp = at("in_tmp", [P, KT, SEQ], R_A + 32 * KIB)
        x_raw = at("x_raw", [P, TB, D], R_A + 32 * KIB)
        x_junk = at("x_junk", [P, D], R_A)
        x1_end = at("x1_end", [P, TB, D], R_A)
        o_junk = at("o_junk", [P, TB, 512], R_A + 32 * KIB)
        xn_t = at("xn_t", [P, KT, SEQ], R_B)
        cat = at("cat", [P, KT, SEQ], R_B)
        x_res = at("x_res", [P, TB, D], R_B)
        hid_hi = at("hid_hi", [P, FT, SEQ], R_B, F32R)
        hid_lo = at("hid_lo", [P, FT, SEQ], R_B + 16 * KIB, F32R)
        hid_tmp = at("hid_tmp", [P, FT, SEQ], R_B + 16 * KIB)
        w_raw = [at(f"w_raw{s}", [P, 2048], R_C + 8 * KIB * s) for s in range(2)]
        w_hi = [at(f"w_hi{s}", [P, 2048], R_C + 8 * KIB * (2 + s), F32R) for s in range(2)]
        w_lo = [at(f"w_lo{s}", [P, 2048], R_C + 8 * KIB * (4 + s), F32R) for s in range(2)]
        grp = at("grp", [P, TILES, SEQ], R_G)
        y = at("y", [P, TB, D], R_G)
        ada1 = [at(f"ada1{u}", [P, KT, P], R_G + 8 * KIB * u) for u in range(2)]
        rows_a = at("rows_a", [6 * KT, P], R_G + 16 * KIB)
        rows_c = at("rows_c", [KT, P], R_B)
        rows_b = at("rows_b", [20, P], R_G + 16 * KIB + 512)
        wm_raw = at("wm_raw", [P, KT, 40], R_T + 8 * KIB)
        wm_hi = at("wm_hi", [P, KT, 40], R_GG, F32R)
        wm_lo = at("wm_lo", [P, KT, 40], R_G + 17 * KIB, F32R)
        f_z = at("f_z", [40, SEQ], R_T + 4 * KIB)
        f_a = at("f_a", [40, SEQ], R_T + 6 * KIB)
        cumb = [at(f"cumb{n}", [P, SEQ], R_T + 2 * KIB * n) for n in range(2)]
        bias = at("bias", [P, SEQ], R_T + 4 * KIB)
        logit = at("logit", [P, SEQ], R_T + 6 * KIB)
        prob = at("prob", [P, SEQ], R_T + 8 * KIB)
        prob_t = at("prob_t", [P, SEQ], R_T + 10 * KIB)
        fv_tok = at("fv_tok", [P, 2, TB, P], R_T + 12 * KIB)
        f_o = at("f_o", [P, P], R_T + 16 * KIB)
        f_junk = at("f_junk", [P, P], R_T + 16 * KIB + 512)
        neg_max, row_max, row_sum, row_inv, f_ms, f_r = [
            at(name, [P, 8], R_T + 17 * KIB + 32 * n) for n, name in enumerate(
                ("neg_max", "row_max", "row_sum", "row_inv", "f_ms", "f_r"))]
        causal = at("causal", [P, P], R_T + 17 * KIB + 256)
        states = at("states", [P, NCH, GLA_DV], R_T)
        g_z = at("g_z", [P, SEQ], R_T)
        g_e = at("g_e", [P, SEQ], R_T + 2 * KIB)
        g_cum = at("g_cum", [P, NCH, CHUNK], R_T + 4 * KIB)
        g_dif = at("g_dif", [P, NCH, CHUNK], R_T + 6 * KIB)
        sig = grp[:, GV0:GV1 + 1, :]
        g_junk = at("g_junk", [P, GLA_DV], R_T + 4 * KIB)
        gv_tok = at("gv_tok", [P, TB, GLA_DV], R_T + 8 * KIB)
        kd_tok = at("kd_tok", [P, TB, P], R_T + 12 * KIB)
        g_o = at("g_o", [P, TB, GLA_DV], R_T + 14 * KIB)
        chunk_on = at("chunk_on", [P, SEQ], R_T + 18 * KIB)
        ada0 = [at(f"ada0{u}", [P, KT, P], R_AD + 8 * KIB * u) for u in range(2)]
        gg = at("gg", [P, D], R_GG)

        k_at = [R_K]

        def small(name, shape):
            t = at(name, shape, k_at[0])
            size = 4
            for n in shape[1:]:
                size *= n
            k_at[0] += (size + 31) // 32 * 32
            return t

        ident = small("ident", [P, P])
        ones = small("ones", [P, P])
        acc = [small("acc0", [P, 2 * P]), at("acc1", [P, 2 * P], R_T + 16 * KIB)]
        bg_bc = small("bg_bc", [P, 2, 2 * P])
        cols_a = small("cols_a", [P, 6 * KT])
        cols_b = small("cols_b", [P, 20])
        mod_a = small("mod_a", [P, KT])
        mod_b = small("mod_b", [P, KT])
        c_act = small("c_act", [P, KT])
        ga_t = small("ga_t", [RANK, SEQ])
        a2h = small("a2h", [RANK, P])
        b_fg = small("b_fg", [40, 1])
        cumq = small("cumq", [P, TB, FOX_HEADS])
        neg_half = small("neg_half", [P, 16])
        ss = small("ss", [P, 16])
        ms = small("ms", [P, 16])
        rstd = small("rstd", [P, 16])
        ss4 = small("ss4", [P, 4])
        ss_x = small("ss_x", [P, 8])
        decay = small("decay", [P, NCH])
        assert k_at[0] <= nc.sbuf_usable_end

        C_GPRE, C_SHM, C_SCM, C_SHF, C_SCF, C_GPRE2 = [KT * n for n in range(6)]
        B_A2, B_GFOX, B_GGLA = 0, GLA_HEADS, GLA_HEADS + FOX_HEADS

        bank = [ctx.enter_context(nc.psum_tensor(f"bank{b}", [P, 512], F32)) for b in range(8)]
        BA, BB = bank[6], bank[7]

        cum_dram = nc.dram_tensor("cum_scratch", (FOX_HEADS, SEQ), F32, kind="Internal").ap()
        x1_dram = nc.dram_tensor("x1_scratch", (SEQ, D), F32, kind="Internal").ap()
        x1_t = x1_dram.rearrange("(t p) d -> p t d", p=P)

        def sem(name):
            return ctx.enter_context(nc.semaphore(name))

        x_in = [sem(f"x_in{t}") for t in range(TB)]
        rows_in = sem("rows_in")
        c_in = sem("c_in")
        bfg_in = sem("bfg_in")
        wm_in = sem("wm_in")
        w_in_s = [sem("w_in0"), sem("w_in1")]
        ada_in = [[sem(f"ada_in{b}{u}") for u in range(2)] for b in range(2)]
        bg_in = sem("bg_in")
        a2_in = sem("a2_in")
        cum_out = sem("cum_out")
        cumb_in = sem("cumb_in")
        xres_in = [sem(f"xres_in{t}") for t in range(TB)]
        x1_out = sem("x1_out")
        x1_in = [sem(f"x1_in{t}") for t in range(TB)]
        out_done = sem("out_done")
        hi_done = sem("hi_done")
        lo_done = sem("lo_done")
        w_used = sem("w_used")
        tile_sum = sem("tile_sum")
        ev_act = sem("ev_act")
        ev_dve = sem("ev_dve")
        consts = sem("consts")
        rows_tr = sem("rows_tr")
        c_tr = sem("c_tr")
        cols_ready = sem("cols_ready")
        ce_ready = sem("ce_ready")
        c_ready = sem("c_ready")
        x_ss = sem("x_ss")
        x_rstd = sem("x_rstd")
        xn_ready = sem("xn_ready")
        x_tr = sem("x_tr")
        xt_act = sem("xt_act")
        xt_dve = sem("xt_dve")
        wm_zero = sem("wm_zero")
        wm_hid = sem("wm_hid")
        wm_lod = sem("wm_lod")
        misc_sum = sem("misc_sum")
        fz_abs = sem("fz_abs")
        fz_ln = sem("fz_ln")
        cum_ready = sem("cum_ready")
        cumq_tr = sem("cumq_tr")
        cumq_ready = sem("cumq_ready")
        ada_mul = [sem("ada_mul_act"), sem("ada_mul_pool")]
        ada_acc = [sem("ada_acc0"), sem("ada_acc1")]
        ada_sum = sem("ada_sum")
        ada_col = sem("ada_col")
        mod_tmp = sem("mod_tmp")
        mod_hi = sem("mod_hi")
        mod_lo = sem("mod_lo")
        fox_v_tr = sem("fox_v_tr")
        fox_v_tok = sem("fox_v_tok")
        fox_qk = sem("fox_qk")
        fox_bias_ready = sem("fox_bias_ready")
        fox_max = sem("fox_max")
        fox_exp = sem("fox_exp")
        fox_p_tr = sem("fox_p_tr")
        fox_p_tok = sem("fox_p_tok")
        fox_pv = sem("fox_pv")
        fox_out = sem("fox_out")
        fox_ss = sem("fox_ss")
        fox_rstd = sem("fox_rstd")
        fox_norm = sem("fox_norm")
        gla_z = sem("gla_z")
        gla_abs = sem("gla_abs")
        gla_ln = sem("gla_ln")
        gla_cum = sem("gla_cum")
        gla_decay = sem("gla_decay")
        gla_kd = sem("gla_kd")
        gla_v_tr = sem("gla_v_tr")
        gla_v_tok = sem("gla_v_tok")
        gla_k_tr = sem("gla_k_tr")
        gla_k_tok = sem("gla_k_tok")
        gla_u = sem("gla_u")
        gla_state = sem("gla_state")
        gla_o = sem("gla_o")
        gla_o_tok = sem("gla_o_tok")
        gla_ss = sem("gla_ss")
        gla_rstd = sem("gla_rstd")
        gla_norm = sem("gla_norm")
        gla_sig_e = sem("gla_sig_e")
        gla_o_tr = sem("gla_o_tr")
        gla_cat = sem("gla_cat")
        cat_hi = sem("cat_hi")
        cat_lo = sem("cat_lo")
        y_sum = sem("y_sum")
        y_sq = sem("y_sq")
        y_mul = sem("y_mul")
        y_rstd = sem("y_rstd")
        y_gate = sem("y_gate")
        x1_ready = sem("x1_ready")
        x1_ss = sem("x1_ss")
        x1_sq = sem("x1_sq")
        xn2_dve = sem("xn2_dve")
        x1_rstd = sem("x1_rstd")
        xn2_ready = sem("xn2_ready")
        h_sum = sem("h_sum")
        h_relu = sem("h_relu")
        h_sq = sem("h_sq")
        h_hi = sem("h_hi")
        h_lo = sem("h_lo")
        y2_sum = sem("y2_sum")
        y2_add = sem("y2_add")
        o_sq = sem("o_sq")
        o_mul = sem("o_mul")
        o_ss = sem("o_ss")
        o_rstd = sem("o_rstd")
        o_ready = sem("o_ready")

        def arrived_group(r, mm):
            return 16 * GROUP_DMAS * (r * (MM_G // 2) + mm // 2 + 1)

        def arrived_out(cg, mm):
            return RAW_OUT + 16 * (cg * (MM_O // 2) + mm // 2 + 1)

        def arrived_mlp(fb, mm):
            return RAW_MLP + 16 * (fb * (MM_F // 2) + mm // 2 + 1)

        NARROW = slice(0, 2 * TILES * P)

        def group_view(t):
            return t[:, 0:2 * TILES * P].rearrange("p (k n) -> p k n", k=2)

        def wide_view(t):
            return t[:, :].rearrange("p (k n) -> p k n", k=4)

        block = ctx.enter_context(nc.Block())

        @block.sync
        def _(sp):
            def slot_free(m):
                sp.wait_ge(hi_done, m - 1)
                sp.wait_ge(lo_done, m - 1)

            def load_fox(r, mm, wait=True):
                if wait:
                    slot_free(r * MM_G + mm)
                dst = group_view(w_raw[mm % 2])
                for k in range(2):
                    src = w_in_t[:, 2 * mm + k, 0:3 * FOX_WIDTH].rearrange("p (s n) -> p s n", s=3)
                    to = dst[:, k, :].rearrange("p (s n) -> p s n", s=3)
                    for part in (slice(0, 2), slice(2, 3)):
                        sp.dma_start(to[:, part, :], src[:, part, bass.ds(r * 2 * P, 2 * P)])\
                            .then_inc(w_in_s[mm % 2], 16)

            def load_gla(h, mm):
                slot_free((FOX_GROUPS + h) * MM_G + mm)
                dst = group_view(w_raw[mm % 2])
                k = slice(2 * mm, 2 * mm + 2)
                for t, col, width in ((GQ, GQ_COL, GLA_DK), (GK, GK_COL, GLA_DK), (GV0, GV_COL, GLA_DV),
                                      (GR0, GR_COL, GLA_DV)):
                    sp.dma_start(dst[:, :, t * P:t * P + width],
                                 w_in_t[:, k, bass.ds(h * width + col, width)]).then_inc(w_in_s[mm % 2], 16)

            def load_out(cg, mm):
                slot_free(M_OUT + cg * MM_O + mm)
                sp.dma_start(wide_view(w_raw[mm % 2]), w_out_t[:, 4 * mm:4 * mm + 4, cg * 512:cg * 512 + 512])\
                    .then_inc(w_in_s[mm % 2], 16)

            def load_m1(fb, half, mm):
                slot_free(M_MLP + fb * MM_F + half * MM_O + mm)
                sp.dma_start(wide_view(w_raw[mm % 2]),
                             w_m1_t[:, 4 * mm:4 * mm + 4, bass.ds(fb * FBLK + half * 512, 512)])\
                    .then_inc(w_in_s[mm % 2], 16)

            def load_m2(fb, cg, mm):
                slot_free(M_MLP + fb * MM_F + 2 * MM_O + cg * 2 + mm)
                sp.dma_start(wide_view(w_raw[mm % 2]),
                             w_m2_t[:, bass.ds(fb * FT + 4 * mm, 4), cg * 512:cg * 512 + 512])\
                    .then_inc(w_in_s[mm % 2], 16)

            def load_ada(summed, col_a, col_b, b):
                for u, col in enumerate((col_a, col_b)):
                    if summed is not None:
                        sp.wait_ge(ada_acc[u], summed)
                    sp.dma_start((ada0, ada1)[b][u][:, :, :], w_ada_t[:, :, bass.ds(col, P)])\
                        .then_inc(ada_in[b][u], 16)

            def load_mod_f(q, k):
                load_ada(q, k * P + SCALE_F, k * P + SHIFT_F, 0)

            def load_gate(q, k, col, g_post):
                load_ada(q, k * 2 * P + col, k * 2 * P + col + P, 0)
                sp.wait_ge(ada_col, q)
                sp.dma_start(bg_bc[:, 0, :], b_ada[0:1, bass.ds(k * 2 * P + col, 2 * P)].to_broadcast([P, 2 * P]))\
                    .then_inc(bg_in, 16)
                sp.dma_start(bg_bc[:, 1, :], g_post[0:1, bass.ds(k * 2 * P, 2 * P)].to_broadcast([P, 2 * P]))\
                    .then_inc(bg_in, 16)

            def as_rows(dst, src, done):
                sp.dma_start(dst, src.rearrange("o (k p) -> (o k) p", p=P)).then_inc(done, 16)

            def load_ada_m(q):
                load_ada(q - 1 if q >= 2 else None, q * P + SCALE_M, q * P + SHIFT_M, q % 2)

            as_rows(rows_c[:, :], c[0:1, :], c_in)
            load_ada_m(0)
            load_ada_m(1)
            for n, src in enumerate((g_pre_mix[0:1, :], b_ada[0:1, SHIFT_M:SHIFT_M + D],
                                     b_ada[0:1, SCALE_M:SCALE_M + D], b_ada[0:1, SHIFT_F:SHIFT_F + D],
                                     b_ada[0:1, SCALE_F:SCALE_F + D], g_pre_mlp[0:1, :])):
                as_rows(rows_a[n * KT:(n + 1) * KT, :], src, rows_in)
            as_rows(rows_b[B_A2:B_GFOX, :], b_gla_a2, rows_in)
            sp.dma_start(rows_b[B_GFOX:B_GGLA, :], g_fox_out[0]).then_inc(rows_in, 16)
            sp.dma_start(rows_b[B_GGLA:20, :], g_gla_out[0].rearrange("h (k p) -> (h k) p", p=P)).then_inc(rows_in, 16)
            for t in range(TB):
                sp.dma_start(x_raw[:, t, :], x_t[:, t, :]).then_inc(x_in[t], 16)
            sp.wait_ge(wm_zero, 1)
            sp.dma_start(wm_raw[:, :, 0:RANK], w_in_t[:, :, GA_COL:GA_COL + RANK]).then_inc(wm_in, 16)
            sp.dma_start(wm_raw[:, :, 32:32 + FOX_HEADS], w_in_t[:, :, FF_COL:FF_COL + FOX_HEADS]).then_inc(wm_in, 16)
            sp.dma_start(b_fg[32:40, :], b_fgate.rearrange("o h -> h o")).then_inc(bfg_in, 16)
            load_fox(0, 0, wait=False)
            load_ada_m(2)
            load_fox(0, 1, wait=False)
            for q in range(3, KT):
                load_ada_m(q)
                if q % 2 and q < KT - 1:
                    load_fox(0, (q + 1) // 2)

            def load_cumb(f):
                sp.wait_ge(ev_act, 3 * f + 1)
                for n in range(2):
                    sp.dma_start(cumb[n][:, :], cum_dram[bass.ds(2 * f + n, 1), :].to_broadcast([P, SEQ]))\
                        .then_inc(cumb_in, 16)

            ADA_AT = {1: 0, 4: 1, 6: 2}

            with sp.Fori(1, FOX_GROUPS) as r:
                for mm in range(MM_G):
                    load_fox(r, mm)
                    if mm == 1:
                        sp.wait_ge(cum_out, 16)
                        load_cumb(r - 1)
                    if mm in ADA_AT:
                        k = (r - 1) * 3 + ADA_AT[mm]
                        load_mod_f(k + Q_FOX, k)
            for mm in range(MM_G):
                load_gla(0, mm)
                if mm == 0:
                    load_cumb(FOX_GROUPS - 1)
                if mm in ADA_AT:
                    k = 3 * (FOX_GROUPS - 1) + ADA_AT[mm]
                    load_mod_f(k + Q_FOX, k)
            with sp.Fori(0, GLA_HEADS - 1) as h:
                for mm in range(MM_G):
                    load_gla(h + 1, mm)
                    if mm == 0:
                        sp.wait_ge(ev_act, 3 * (FOX_GROUPS + h) + 1)
                        sp.dma_start(a2h[:, :], w_gla_a2[0, :, bass.ds(h * P, P)]).then_inc(a2_in, 16)
                    if mm in ADA_AT:
                        j = ADA_AT[mm]
                        if j == 0:
                            load_mod_f(h * 3 + Q_GLA, h + 3 * FOX_GROUPS)
                        else:
                            load_gate(h * 3 + (Q_GLA + j), h * 2 + (j - 1), GATE_M, g_post_mix)
            sp.wait_ge(gla_z, GLA_HEADS - 1)
            sp.dma_start(a2h[:, :], w_gla_a2[0, :, (GLA_HEADS - 1) * P:GLA_HEADS * P]).then_inc(a2_in, 16)
            for cg in range(CG):
                for mm in range(MM_O):
                    load_out(cg, mm)
                    if cg == 0 and mm == 0:
                        load_mod_f(Q_GF - 3, KT - 1)
                    if cg in (1, 2) and mm == 0:
                        load_gate(Q_GF - 3 + cg, KT // 2 - 3 + cg, GATE_M, g_post_mix)
                if cg == 1:
                    sp.wait_ge(cat_hi, KT)
                    sp.wait_ge(cat_lo, KT)
                    for t in range(TB):
                        sp.dma_start(x_res[:, t, :], x_t[:, t, :]).then_inc(xres_in[t], 16)
            with sp.Fori(0, FBS) as fb:
                for half in range(2):
                    for mm in range(MM_O):
                        load_m1(fb, half, mm)
                        if half == 0 and mm == 2:
                            load_gate(fb + Q_GF, fb, GATE_F, g_post_mlp)
                for cg in range(CG):
                    for mm in range(2):
                        load_m2(fb, cg, mm)
            sp.wait_ge(x1_out, 16 * TB)
            sp.wait_ge(w_used, M_MLP + (FBS - 1) * MM_F + 2 * MM_O)
            for t in range(TB):
                sp.dma_start(x1_end[:, t, :], x1_t[:, t, :]).then_inc(x1_in[t], 16)
            for t in range(TB):
                if t < TB - 1:
                    sp.wait_ge(o_ready, t + 1)
                    sp.dma_start(out_t[:, t, :], x1_end[:, t, :]).then_inc(out_done, 16)
            for half in range(2):
                sp.wait_ge(o_ready, TB + half)
                cols = slice(half * D // 2, (half + 1) * D // 2)
                sp.dma_start(out_t[:, TB - 1, cols], x1_end[:, TB - 1, cols]).then_inc(out_done, 16)
            sp.wait_ge(out_done, 16 * (TB + 1))

        @block.tensor
        def _(pe):
            def split_mm(dst, a, b, start, stop):
                pe.matmul(dst, a[0], b[0], start=start, stop=False)
                pe.matmul(dst, a[0], b[1], start=False, stop=False)
                return pe.matmul(dst, a[1], b[0], start=False, stop=stop)

            def group_steps(r, first, slot, misc_step=None):
                for k in range(KT):
                    s, m = (k // 2) % 2, r * MM_G + k // 2
                    hi, lo = group_view(w_hi[s])[:, k % 2, :], group_view(w_lo[s])[:, k % 2, :]
                    if first:
                        slot(2 * k)
                    if k % 2 == 0:
                        pe.wait_ge(hi_done, m + 1)
                        pe.wait_ge(lo_done, m + 1)
                    if first:
                        pe.wait_ge(mod_lo, k + 1)
                        misc_step(k)
                    for b in range(TILES):
                        if k == 0 and not first:
                            pe.wait_ge((ev_act, ev_dve)[b % 2], r * 3 - 2 + b // 2)
                        cols = slice(b * P, b * P + P)
                        last = split_mm(bank[b][:, :], (hi[:, cols], lo[:, cols]),
                                        (in_hi[:, k, :], in_lo[:, k, :]), k == 0, k == KT - 1)
                        if k == KT - 1 and b < TILES - 1:
                            last.then_inc(tile_sum, 1)
                        if b == TILES - 1 and k % 2:
                            last.then_inc(w_used, 1)
                        if not first and b == 2:
                            slot(2 * k)
                    if not first:
                        slot(2 * k + 1)

            def ada_columns(q, dst, a=0):
                pe.wait_ge(ada_acc[0], q + 1)
                pe.wait_ge(ada_acc[1], q + 1)
                pe.matmul(dst[:, 0:1], acc[a][:, 0:P], ones[:, 0:1], start=True, stop=True)
                pe.matmul(dst[:, 1:2], acc[a][:, P:2 * P], ones[:, 0:1], start=True, stop=True).then_inc(ada_sum, 1)

            def ada_rows(q, dst):
                pe.wait_ge(ada_acc[0], q + 1)
                pe.wait_ge(ada_acc[1], q + 1)
                pe.matmul(dst[:, 0:2 * P], ones[:, :], acc[0][:, :], start=True, stop=True).then_inc(ada_sum, 1)

            def fox_slot(s, f):
                if s == 0:
                    pe.wait_ge(ev_act, 3 * f + 3)
                    pe.wait_ge(ev_dve, 3 * f + 3)
                    for t in range(TB):
                        last = pe.transpose(BB[:, t * P:t * P + P], grp[:, VA, t * P:t * P + P], ident[:, :])
                    last.then_inc(fox_v_tr, 1)
                if s == 1:
                    pe.wait_ge(fox_max, 8 * f + 1)
                    for t in range(TB):
                        last = pe.transpose(BA[:, t * P:t * P + P], grp[:, VB, t * P:t * P + P], ident[:, :])
                    last.then_inc(fox_v_tr, 1)
                if s % 3 == 0 and s // 3 < 8:
                    j = s // 3
                    i = j % TB
                    if j:
                        pe.wait_ge(fox_max, 8 * f + j)
                    if j == 1:
                        pe.wait_ge(fox_v_tok, 2 * f + 2)
                    if j == 0:
                        pe.wait_ge(ada_col, 3 * f + Q_FOX)
                    q_tile, k_tile = (QA, KA) if j < TB else (QB, KB)
                    pe.matmul(BA[:, 0:(i + 1) * P], grp[:, q_tile, i * P:i * P + P], grp[:, k_tile, 0:(i + 1) * P],
                              start=True, stop=True).then_inc(fox_qk, 1)
                if s % 3 == 2 and s // 3 < 8:
                    j = s // 3
                    pe.wait_ge(fox_exp, 8 * f + j + 1)
                    if j == 0:
                        pe.wait_ge(fox_v_tok, 2 * f + 1)
                    else:
                        pe.wait_ge(fox_out, 9 * f + j)
                    for t in range(j % TB + 1):
                        last = pe.transpose(BB[:, t * P:t * P + P], prob[:, t * P:t * P + P], ident[:, :])
                    last.then_inc(fox_p_tr, 1)
                if s % 3 == 1 and 4 <= s <= 25:
                    j = (s - 4) // 3
                    i = j % TB
                    pe.wait_ge(fox_p_tok, 8 * f + j + 1)
                    if j == 0:
                        pe.wait_ge(fox_v_tok, 2 * f + 2)
                    else:
                        fox_out_transpose(f, j - 1)
                    for t in range(i + 1):
                        last = pe.matmul(BB[:, 0:P], prob_t[:, t * P:t * P + P], fv_tok[:, j // TB, t, :],
                                         start=(t == 0), stop=(t == i))
                    last.then_inc(fox_pv, 1)
                if s == 28:
                    pe.wait_ge(fox_out, 9 * f + 8)
                    fox_out_transpose(f, 7).then_inc(fox_pv, 1)

            def fox_out_transpose(f, j):
                pe.wait_ge(fox_norm, 8 * f + j + 1)
                return pe.transpose(BB[:, P:2 * P], f_o[:, :], ident[:, :])

            def gla_slot(s, h, ada, last_head=False):
                if s == 0:
                    pe.wait_ge(ev_act, 3 * (h + FOX_GROUPS) + 3)
                    pe.wait_ge(ev_dve, 3 * (h + FOX_GROUPS) + 3)
                    pe.wait_ge(a2_in, 16 * (h + 1))
                    pe.wait_ge(fox_out, 9 * FOX_GROUPS)
                    pe.wait_ge(fox_max, 8 * FOX_GROUPS)
                    pe.wait_ge(ada_col, ada)
                    pe.matmul(BA[:, :], a2h[:, :], ga_t[:, :], start=True, stop=True).then_inc(gla_z, 1)
                if s in (1, 3):
                    if s == 3:
                        pe.wait_ge(gla_v_tok, 2 * h + 1)
                    for t in range(TB):
                        last = pe.transpose(BB[:, t * P:t * P + P], grp[:, GV0 + s // 2, t * P:t * P + P], ident[:, :])
                    last.then_inc(gla_v_tr, 1)
                if s == 7:
                    pe.wait_ge(gla_kd, h + 1)
                    for t in range(TB):
                        last = pe.transpose(BA[:, t * P:t * P + P], g_e[:, t * P:t * P + P], ident[:, :])
                    last.then_inc(gla_k_tr, 1)
                if s == 12:
                    pe.wait_ge(gla_state, 2 * h + 1)
                    ada_columns(ada, BB)
                if s in (10, 13):
                    if s == 10:
                        pe.wait_ge(gla_k_tok, h + 1)
                    else:
                        pe.wait_ge(ada_col, ada + 1)
                    for n in range(4):
                        t, rows = (n + 4 * (s == 13)) // 2, slice(CHUNK * (n % 2), CHUNK * (n % 2) + CHUNK)
                        last = pe.matmul((BA, BB)[n % 2][:, (n // 2) * GLA_DV:(n // 2 + 1) * GLA_DV],
                                         kd_tok[rows, t, :], gv_tok[rows, t, :], start=True, stop=True)
                    last.then_inc(gla_u, 1)
                if s in (16, 17):
                    if s == 16:
                        pe.wait_ge(gla_state, 2 * h + 2)
                    for n in range(4):
                        ch = n + 4 * (s == 17)
                        rows = slice(CHUNK * (n % 2), CHUNK * (n % 2) + CHUNK)
                        last = pe.matmul((BA, BB)[s - 16][rows, (n // 2) * GLA_DV:(n // 2 + 1) * GLA_DV],
                                         grp[:, GQ, ch * CHUNK:ch * CHUNK + CHUNK], states[:, ch, :],
                                         start=True, stop=True)
                    last.then_inc(gla_o, 1)
                if s == 20 and not last_head:
                    pe.wait_ge(gla_o_tok, 2 * h + 1)
                    ada_rows(ada + 1, BA)
                if s in (23, 24):
                    if s == 23:
                        pe.wait_ge(gla_norm, h + 1)
                        if not last_head:
                            pe.wait_ge(ada_col, ada + 2)
                    half = s - 23
                    for t in range(TB):
                        last = pe.transpose((BA, BB)[half][:, t * P:t * P + P],
                                            g_o[:, t, half * P:half * P + P], ident[:, :])
                    last.then_inc(gla_o_tr, 1)
                if s == 30 and not last_head:
                    pe.wait_ge(gla_cat, 2 * h + 1)
                    ada_rows(ada + 2, BA)

            pe.wait_ge(consts, 1)
            pe.wait_ge(c_in, 16)
            pe.transpose(BB[:, 0:KT], rows_c[:, :], ident[0:KT, 0:KT]).then_inc(c_tr, 1)
            pe.wait_ge(rows_in, 16 * 9)
            pe.transpose(BA[:, 0:6 * KT], rows_a[:, :], ident[0:6 * KT, 0:6 * KT])
            pe.transpose(BA[:, 128:148], rows_b[:, :], ident[0:20, 0:20]).then_inc(rows_tr, 1)
            for k in range(KT):
                if k == 0:
                    pe.wait_ge(xn_ready, TB)
                if k >= TILES:
                    pe.wait_ge((xt_act, xt_dve)[k % 2], (k - TILES) // 2 + 1)
                for t in range(TB):
                    last = pe.transpose(bank[k % TILES][:, t * P:t * P + P], x_raw[:, t, k * P:k * P + P], ident[:, :])
                last.then_inc(x_tr, 1)

            def start_slot(s):
                if s == 0:
                    pe.wait_ge(xt_act, KT // 2)
                    pe.wait_ge(xt_dve, KT // 2)
                    pe.wait_ge(cols_ready, 1)
                    pe.wait_ge(c_ready, 1)
                    ada_columns(0, BA[:, 0:2], 0)
                if s % 2 == 0 and s // 2 + 1 < KT:
                    q = s // 2 + 1
                    pe.wait_ge(ada_col, q)
                    ada_columns(q, BA[:, 0:2], q % 2)

            def misc_step(k):
                if k == 0:
                    pe.wait_ge(wm_hid, 1)
                    pe.wait_ge(wm_lod, 1)
                last = split_mm(BB[0:40, :], (wm_hi[:, k, :], wm_lo[:, k, :]), (in_hi[:, k, :], in_lo[:, k, :]),
                                k == 0, k == KT - 1)
                if k == KT - 1:
                    last.then_inc(misc_sum, 1)

            group_steps(0, True, start_slot, misc_step)

            FOX_ADA = {14: 0, 23: 1, 31: 2}

            def fox_ada_slot(s, f):
                if s in FOX_ADA:
                    j = min(s // 3, 7)
                    pe.wait_ge(fox_max, 8 * f + j + 1)
                    ada_columns(3 * f + (FOX_ADA[s] + Q_FOX), BA)

            def fox_slots(f):
                def slot(s):
                    if s - 1 in FOX_ADA:
                        pe.wait_ge(ada_col, 3 * f + (FOX_ADA[s - 1] + Q_FOX + 1))
                    fox_slot(s, f)
                    fox_ada_slot(s, f)
                return slot

            pe.wait_ge(cum_ready, 1)
            for t in range(TB):
                last = pe.transpose(BA[:, t * FOX_HEADS:(t + 1) * FOX_HEADS], f_z[32:40, t * P:t * P + P],
                                    ident[32:40, 32:40])
            last.then_inc(cumq_tr, 1)
            pe.wait_ge(cumq_ready, 1)
            with pe.Fori(1, FOX_GROUPS) as r:
                group_steps(r, False, fox_slots(r - 1))
            group_steps(FOX_GROUPS, False, fox_slots(FOX_GROUPS - 1))
            with pe.Fori(0, GLA_HEADS - 1) as h:
                group_steps(h + (FOX_GROUPS + 1), False, lambda s: gla_slot(s, h, h * 3 + Q_GLA))

            def out_steps(cg):
                steps = [(k, t) for k in range(KT) for t in range(TB)]
                if cg == CG - 1:
                    steps = steps[:KT * TB // 2] + [(k, t) for t in range(TB) for k in range(KT // 2, KT)]
                for k, t in steps:
                    s, m = (k // 4) % 2, M_OUT + cg * MM_O + k // 4
                    hi, lo = wide_view(w_hi[s])[:, k % 4, :], wide_view(w_lo[s])[:, k % 4, :]
                    if t == 0 and k % 4 == 0:
                        pe.wait_ge(hi_done, m + 1)
                        pe.wait_ge(lo_done, m + 1)
                    if t == 0 and cg == 0:
                        pe.wait_ge(cat_lo, k + 1)
                    if k == 0:
                        if cg == 0:
                            pe.wait_ge((ev_act, ev_dve)[t % 2], GROUPS * 3 - 2 + t // 2)
                        elif cg == 1:
                            pe.wait_ge(ev_act, GROUPS * 3)
                            pe.wait_ge(ev_dve, GROUPS * 3)
                            pe.wait_ge(gla_cat, 2 * GLA_HEADS)
                        else:
                            pe.wait_ge(y_mul, (cg - 2) * TB + t + 1)
                            if t == TB - 1:
                                pe.wait_ge(ada_col, Q_GF - 3 + cg)
                    cols = slice(t * P, t * P + P)
                    last = split_mm(bank[4 * (cg % 2) + t][:, :], (in_hi[:, k, cols], in_lo[:, k, cols]), (hi, lo),
                                    k == 0, k == KT - 1)
                    if k == KT - 1 and t < TB - 1:
                        last.then_inc(y_sum, 1)
                    if t == TB - 1 and k % 4 == 3:
                        last.then_inc(w_used, 1)
                    if cg in (1, 2) and k == KT - 2 and t == 0:
                        pe.wait_ge(y_mul, cg * TB)
                        ada_rows(Q_GF - 3 + cg, bank[(3, 7)[cg - 1]])
                    if cg == 0 and t % 2 == 1:
                        gla_slot(2 * k + t // 2, GLA_HEADS - 1, Q_GF - 3, True)

            for cg in range(CG):
                out_steps(cg)

            def x1_transpose(k):
                if k >= 4:
                    pe.wait_ge(mod_tmp, KT + k - 3)
                for t in range(TB):
                    last = pe.transpose(bank[4 + k % 4][:, t * P:t * P + P], y[:, t, k * P:k * P + P], ident[:, :])
                last.then_inc(x_tr, 1)

            pe.wait_ge(xn2_ready, 1)
            pe.wait_ge(xn2_dve, TB - 1)
            pe.wait_ge(y_mul, CG * TB)
            for k in range(4):
                x1_transpose(k)

            def mlp_block(fb, first=False, last_block=False):
                for half in range(2):
                    for k in range(KT):
                        s, m = (k // 4) % 2, M_MLP + fb * MM_F + half * MM_O + k // 4
                        hi, lo = wide_view(w_hi[s])[:, k % 4, :], wide_view(w_lo[s])[:, k % 4, :]
                        if k % 4 == 0:
                            pe.wait_ge(hi_done, m + 1)
                            pe.wait_ge(lo_done, m + 1)
                        if first and half == 0:
                            pe.wait_ge(mod_lo, KT + k + 1)
                        for b in range(4):
                            if k == 0:
                                if half == 1:
                                    pe.wait_ge(h_relu, fb * FT + b + 1)
                            last = split_mm(bank[b][:, :], (hi[:, b * P:b * P + P], lo[:, b * P:b * P + P]),
                                            (in_hi[:, k, :], in_lo[:, k, :]), k == 0, k == KT - 1)
                            if k == KT - 1 and b < 3:
                                last.then_inc(h_sum, 1)
                            if half == 1 and k == KT - 2 and b == 0:
                                pe.wait_ge(y2_add, fb * 16 + 1)
                                ada_rows(fb + Q_GF, bank[7])
                        if k % 4 == 3:
                            last.then_inc(w_used, 1)
                        if first and half == 0 and k + 4 < KT:
                            x1_transpose(k + 4)
                for cg in range(CG - 1 if last_block else CG):
                    for k in range(FT):
                        s, m = (k // 4) % 2, M_MLP + fb * MM_F + 2 * MM_O + cg * 2 + k // 4
                        hi, lo = wide_view(w_hi[s])[:, k % 4, :], wide_view(w_lo[s])[:, k % 4, :]
                        if k % 4 == 0:
                            pe.wait_ge(hi_done, m + 1)
                            pe.wait_ge(lo_done, m + 1)
                        if cg == 0:
                            pe.wait_ge(h_lo, fb * FT + k + 1)
                        for t in range(TB):
                            if k == 0:
                                if cg:
                                    pe.wait_ge(y2_add, fb * 16 + cg * 4 - 2 + t)
                                else:
                                    pe.wait_ge(y2_add, fb * 16 + 1)
                                if cg == 0 and t == 3:
                                    pe.wait_ge(ada_col, fb + Q_GF + 1)
                            cols = slice(t * P, t * P + P)
                            last = split_mm(bank[4 + t][:, :], (hid_hi[:, k, cols], hid_lo[:, k, cols]), (hi, lo),
                                            k == 0, k == FT - 1)
                            if k == FT - 1 and t < TB - 1:
                                last.then_inc(y2_sum, 1)
                        if k % 4 == 3:
                            last.then_inc(w_used, 1)

                if last_block:
                    cg, m = CG - 1, M_MLP + fb * MM_F + MM_F - 2
                    for t in range(TB):
                        cols = slice(t * P, t * P + P)
                        pe.wait_ge(y2_add, fb * 16 + cg * 4 - 2 + t)
                        for k in range(FT):
                            s = k // 4
                            if k % 4 == 0:
                                pe.wait_ge(hi_done, m + s + 1)
                                pe.wait_ge(lo_done, m + s + 1)
                            hi, lo = wide_view(w_hi[s])[:, k % 4, :], wide_view(w_lo[s])[:, k % 4, :]
                            last = split_mm(bank[4 + t][:, :], (hid_hi[:, k, cols], hid_lo[:, k, cols]), (hi, lo),
                                            k == 0, k == FT - 1)
                            if t == TB - 1 and k % 4 == 3:
                                last.then_inc(w_used, 1)
                        if t < TB - 1:
                            last.then_inc(y2_sum, 1)

            mlp_block(0, first=True)
            with pe.Fori(1, FBS - 1) as fb:
                mlp_block(fb)
            mlp_block(FBS - 1, last_block=True)

        @block.scalar
        def _(act):
            def split_hi(m, arrived, n, view=slice(0, 2048)):
                act.wait_ge(w_in_s[n], arrived)
                act.wait_ge(w_used, m - 1)
                act.activation(w_hi[n][:, view], w_raw[n][:, view], ACT.Copy).then_inc(hi_done, 1)


            def next_hi_group(r, mm, last):
                if mm + 1 < MM_G or not last:
                    split_hi(r * MM_G + (mm + 1), arrived_group(r, mm + 1), (mm + 1) % 2, NARROW)

            def evict_group(r, scaled):
                for b in range(0, TILES, 2):
                    act.wait_ge(tile_sum, r * (TILES - 1) + b + 1)
                    act.activation(grp[:, b, :], bank[b][:, :], ACT.Copy,
                                   scale=FOX_DIM ** -0.5 if scaled and b == QA else 1.0).then_inc(ev_act, 1)

            def ada_times_c(q, half, b=0, arrived=None):
                if half == 0:
                    act.wait_ge(ada_in[b][0], 16 * (q - Q_FOX + KT // 2 + 1) if arrived is None else arrived)
                for k in range(half * KT // 2, (half + 1) * KT // 2):
                    last = act.activation((ada0, ada1)[b][0][:, k, :], (ada0, ada1)[b][0][:, k, :], ACT.Copy,
                                          scale=c_act[:, k:k + 1])
                if half:
                    last.then_inc(ada_mul[0], 1)

            ADA_TIMES = {5: (0, 0), 6: (0, 1), 14: (1, 0), 15: (1, 1), 24: (2, 0), 26: (2, 1)}

            def fox_tiles_free(f):
                act.wait_ge(fox_qk, 8 * f + 8)
                act.wait_ge(fox_v_tr, 2 * f + 2)

            def gla_tiles_free(h):
                act.wait_ge(gla_o, 2 * h + 2)
                act.wait_ge(gla_kd, h + 1)
                act.wait_ge(gla_v_tr, 2 * h + 2)
                act.wait_ge(gla_cat, 2 * h + 2)

            def fox_slot(s, f):
                if s == 0:
                    act.wait_ge(cumb_in, 32 * (f + 1))
                    fox_bias(f, 0)
                if s == 1:
                    act.wait_ge(fox_v_tr, 2 * f + 1)
                    act.activation(fv_tok[:, 0, :, :], BB[:, :].rearrange("p (t d) -> p t d", t=TB), ACT.Copy)\
                        .then_inc(fox_v_tok, 1)
                    act.wait_ge(fox_v_tr, 2 * f + 2)
                    act.activation(fv_tok[:, 1, :, :], BA[:, :].rearrange("p (t d) -> p t d", t=TB), ACT.Copy)\
                        .then_inc(fox_v_tok, 1)
                if s % 3 == 1 and s // 3 < 8:
                    j = s // 3
                    n = (j % TB + 1) * P
                    act.wait_ge(fox_max, 8 * f + j + 1)
                    if j:
                        act.wait_ge(fox_p_tr, 8 * f + j)
                    act.activation(prob[:, 0:n], logit[:, 0:n], ACT.Exp, bias=neg_max[:, j:j + 1],
                                   accum_out=row_sum[:, j:j + 1]).then_inc(fox_exp, 1)
                if s % 3 == 2 and s // 3 < 7:
                    fox_bias(f, s // 3 + 1)
                if s % 3 == 0 and 3 <= s <= 24:
                    j = s // 3 - 1
                    n = (j % TB + 1) * P
                    act.wait_ge(fox_p_tr, 8 * f + j + 1)
                    if j:
                        act.wait_ge(fox_pv, 9 * f + j)
                    act.activation(prob_t[:, 0:n], BB[:, 0:n], ACT.Copy).then_inc(fox_p_tok, 1)

            def fox_bias(f, j):
                i, head = j % TB, 2 * f + j // TB
                if j:
                    act.wait_ge(fox_max, 8 * f + j)
                act.activation(bias[:, 0:(i + 1) * P], cumb[j // TB][:, 0:(i + 1) * P], ACT.Identity,
                               scale=-1.0, bias=cumq[:, i, bass.ds(head, 1)]).then_inc(fox_bias_ready, 1)

            def gla_slot(s, h):
                if s == 2:
                    act.wait_ge(gla_abs, h + 1)
                    act.activation(g_e[:, :], g_e[:, :], ACT.Exp)
                    act.drain()
                    act.activation(g_e[:, :], g_e[:, :], ACT.Ln, bias=1.0).then_inc(gla_ln, 1)
                if s in (2, 4):
                    half = s // 2 - 1
                    act.wait_ge(gla_v_tr, 2 * h + s // 2)
                    act.activation(gv_tok[:, :, half * P:half * P + P],
                                   BB[:, :].rearrange("p (t d) -> p t d", t=TB), ACT.Copy).then_inc(gla_v_tok, 1)
                if s == 5:
                    act.wait_ge(gla_cum, h + 1)
                    act.activation(g_dif[:, :, :], g_dif[:, :, :], ACT.Exp, scale=1.0 / GATE_TEMP)
                    act.activation(decay[:, :], g_cum[:, :, CHUNK - 1], ACT.Exp, scale=1.0 / GATE_TEMP)\
                        .then_inc(gla_decay, 1)
                    act.activation(sig, grp[:, GR0:GR1 + 1, :], ACT.Exp, scale=-1.0).then_inc(gla_sig_e, 1)
                if s == 8:
                    act.wait_ge(gla_k_tr, h + 1)
                    act.activation(kd_tok[:, :, :], BA[:, :].rearrange("p (t d) -> p t d", t=TB), ACT.Copy)\
                        .then_inc(gla_k_tok, 1)
                if s in (17, 18):
                    n = s - 17
                    act.wait_ge(gla_o, 2 * h + n + 1)
                    act.activation(g_o[:, 2 * n:2 * n + 2, :],
                                   (BA, BB)[n][:, :].rearrange("p (t d) -> p t d", t=2), ACT.Copy,
                                   scale=GLA_DK ** -0.5).then_inc(gla_o_tok, 1)

            act.wait_ge(c_tr, 1)
            act.activation(c_act[:, :], BB[:, 0:KT], ACT.Exp, scale=-1.0).then_inc(ce_ready, 1)
            act.wait_ge(c_ready, 1)

            def ada_m_times_c(q):
                ada_times_c(q, 0, q % 2, 16 * (q // 2 + 1))
                ada_times_c(q, 1, q % 2)

            ada_m_times_c(0)
            ada_m_times_c(1)
            for t in range(TB):
                act.wait_ge(x_in[t], 16)
                if t:
                    act.drain()
                act.activation(x_junk[:, :], x_raw[:, t, :], ACT.Square, accum_out=ss[:, t:t + 1]).then_inc(x_ss, 1)
            for k in range(0, KT, 2):
                act.wait_ge(x_tr, k + 1)
                act.activation(xn_t[:, k, :], bank[k % TILES][:, :], ACT.Copy).then_inc(xt_act, 1)
            act.wait_ge(x_tr, KT)
            act.wait_ge(xt_dve, KT // 2)

            def first_hi(m):
                act.wait_ge(w_in_s[m], arrived_group(0, m))
                act.activation(w_hi[m][:, NARROW], w_raw[m][:, NARROW], ACT.Copy).then_inc(hi_done, 1)

            def modulate(k):
                act.wait_ge(ada_col, k + 1)
                act.activation(in_tmp[:, k, :], xn_t[:, k, :], ACT.Identity, scale=mod_a[:, k:k + 1],
                               bias=mod_b[:, k:k + 1]).then_inc(mod_tmp, 1)
                act.wait_ge(mod_tmp, k + 1)
                act.activation(in_hi[:, k, :], in_tmp[:, k, :], ACT.Copy).then_inc(mod_hi, 1)

            act.wait_ge(wm_in, 32)
            act.activation(wm_hi[:, :, :], wm_raw[:, :, :], ACT.Copy).then_inc(wm_hid, 1)
            first_hi(0)
            modulate(0)
            for q in range(2, KT):
                ada_m_times_c(q)
                if q == 2:
                    first_hi(1)
                modulate(q - 1)
                if q % 2 == 0 and q >= 4:
                    split_hi(q // 2, arrived_group(0, q // 2), q // 2 % 2, NARROW)
            modulate(KT - 1)
            act.wait_ge(fz_abs, 1)
            act.activation(f_a[32:40, :], f_a[32:40, :], ACT.Exp)
            act.drain()
            act.activation(f_a[32:40, :], f_a[32:40, :], ACT.Ln, bias=1.0).then_inc(fz_ln, 1)
            split_hi(MM_G, arrived_group(1, 0), 0, NARROW)
            evict_group(0, True)
            act.wait_ge(cum_ready, 1)
            act.dma_start(cum_dram, f_z[32:40, :]).then_inc(cum_out, 16)
            act.wait_ge(cumq_tr, 1)
            act.activation(cumq[:, :, :], BA[:, 0:TB * FOX_HEADS].rearrange("p (t h) -> p t h", t=TB), ACT.Copy)\
                .then_inc(cumq_ready, 1)
            act.wait_ge(cumq_ready, 1)

            def cat_half(k):
                if k < 12:
                    act.wait_ge(w_used, (GROUPS - 1) * MM_G + k // 2 + 1)
                    if k == 0:
                        act.wait_ge(fox_out, 9 * FOX_GROUPS)
                    if k >= FOX_HEADS:
                        act.wait_ge(gla_cat, k + 1 - FOX_HEADS)
                act.activation(in_hi[:, k, :], cat[:, k, :], ACT.Copy).then_inc(cat_hi, 1)

            CAT_AT = {4 * (k // 2 + 1) + 2 + k % 2: k for k in range(12)}

            def group(r, work, q, last=False):
                for s in range(4 * MM_G):
                    work(s)
                    if last and s in CAT_AT:
                        cat_half(CAT_AT[s])
                    if s in ADA_TIMES:
                        ada_times_c(q + ADA_TIMES[s][0], ADA_TIMES[s][1])
                    if s % 4 == 0:
                        next_hi_group(r, s // 4, last)

            with act.Fori(1, FOX_GROUPS) as r:
                group(r, lambda s: fox_slot(s, r - 1), 3 * r + (Q_FOX - 3))
                fox_tiles_free(r - 1)
                evict_group(r, True)
            group(FOX_GROUPS, lambda s: fox_slot(s, FOX_GROUPS - 1), Q_GLA - 3)
            fox_tiles_free(FOX_GROUPS - 1)
            evict_group(FOX_GROUPS, False)

            def gla_group(h, last=False):
                group(h + (FOX_GROUPS + 1), lambda s: gla_slot(s, h), h * 3 + Q_GLA, last)
                if last:
                    split_hi(M_OUT, arrived_out(0, 0), 0)
                gla_tiles_free(h)
                evict_group(h + (FOX_GROUPS + 1), False)

            with act.Fori(0, GLA_HEADS - 2) as h:
                gla_group(h)
            gla_group(GLA_HEADS - 2, last=True)

            act.wait_ge(w_used, M_OUT)
            act.wait_ge(gla_cat, 2 * (GLA_HEADS - 1))
            for k in (KT - 4, KT - 3):
                cat_half(k)
            for s in range(2 * KT):
                gla_slot(s, GLA_HEADS - 1)
                if s in (5, 6):
                    ada_times_c(Q_GF - 3, s - 5)
                if s % 8 == 2 and s // 8 + 1 < MM_O:
                    split_hi(M_OUT + s // 8 + 1, arrived_out(0, s // 8 + 1), (s // 8 + 1) % 2)
                if s == 27:
                    for k in (KT - 2, KT - 1):
                        act.wait_ge(gla_cat, 2 * GLA_HEADS - KT + k + 1)
                        cat_half(k)

            def square_y(cg, t):
                if t < TB - 1:
                    act.wait_ge(y_sum, cg * (TB - 1) + t + 1)
                else:
                    act.wait_ge(w_used, M_OUT + cg * MM_O + MM_O)
                act.activation(y[:, t, cg * 512:cg * 512 + 512], bank[4 * (cg % 2) + t][:, :], ACT.Square,
                               accum_out=ss[:, t * CG + cg:t * CG + cg + 1]).then_inc(y_sq, 1)

            def split_hi_out(m):
                split_hi(M_OUT + m, RAW_OUT + 16 * (m // 2 + 1), m % 2)

            def square_x1(t, half=None):
                cols = slice(0, D) if half is None else slice(half * D // 2, (half + 1) * D // 2)
                act.wait_ge(x1_ready, t + 1 + (half or 0))
                act.activation(y[:, t, cols], x_res[:, t, cols], ACT.Square,
                               accum_out=ss_x[:, t + (half or 0):t + 1 + (half or 0)]).then_inc(x1_ss, 1)

            for cg in range(CG):
                if cg:
                    for mm in range(2, MM_O):
                        split_hi_out(cg * MM_O + mm)
                        if cg < 3:
                            ada_times_c(Q_GF - 3 + cg, mm - 2)
                if cg < CG - 1:
                    split_hi_out(cg * MM_O + MM_O)
                    for t in range(TB):
                        square_y(cg, t)
                    split_hi_out(cg * MM_O + MM_O + 1)

            square_y(CG - 1, 0)
            square_y(CG - 1, 1)
            square_x1(0)
            act.wait_ge(x1_rstd, 1)
            act.activation(y[:, 0, :], x_res[:, 0, :], ACT.Copy, scale=rstd[:, 4:5]).then_inc(xn2_ready, 1)
            square_y(CG - 1, 2)
            square_x1(1)
            split_hi_out(CG * MM_O)
            square_y(CG - 1, TB - 1)
            square_x1(2)
            square_x1(TB - 1, 0)
            square_x1(TB - 1, 1)
            split_hi_out(CG * MM_O + 1)
            for t in range(TB):
                act.dma_start(x1_t[:, t, :], x_res[:, t, :]).then_inc(x1_out, 16)
            for k in range(KT):
                act.wait_ge(mod_tmp, KT + k + 1)
                act.activation(in_hi[:, k, :], in_tmp[:, k, :], ACT.Copy).then_inc(mod_hi, 1)
                if k in (7, 11):
                    split_hi_out(CG * MM_O + k // 4 + 1)
            act.wait_ge(x1_out, 16 * TB)

            def hidden(fb, half):
                def relu(b):
                    if b < 3:
                        act.wait_ge(h_sum, fb * 6 + half * 3 + b + 1)
                    else:
                        act.wait_ge(w_used, M_MLP + fb * MM_F + half * MM_O + MM_O)
                    act.activation(hid_tmp[:, half * 4 + b, :], bank[b][:, :], ACT.Relu).then_inc(h_relu, 1)

                def hi(b):
                    act.wait_ge(h_sq, fb * FT + half * 4 + b + 1)
                    act.activation(hid_hi[:, half * 4 + b, :], hid_tmp[:, half * 4 + b, :], ACT.Copy).then_inc(h_hi, 1)

                act.wait_ge(w_used, M_MLP + fb * MM_F)
                for b in range(4):
                    relu(b)
                mm = (half + 1) * MM_O + 1
                split_hi(M_MLP + fb * MM_F + mm, arrived_mlp(fb, mm), mm % 2)
                for b in range(4):
                    hi(b)

            def square_y2(cg):
                act.drain()
                for t in range(TB):
                    act.wait_ge(y2_add, FBS * 16 - 14 + cg * TB + t)
                    act.activation(o_junk[:, t, :], y[:, t, cg * 512:cg * 512 + 512], ACT.Square,
                                   accum_out=ss[:, t * CG + cg:t * CG + cg + 1]).then_inc(o_sq, 1)

            def mlp_block(fb, first=False, last=False):
                for mm in range(MM_O if first else 0, MM_F):
                    if mm not in (MM_O + 1, 2 * MM_O + 1):
                        split_hi(M_MLP + fb * MM_F + mm, arrived_mlp(fb, mm), mm % 2)
                    if mm == MM_O:
                        hidden(fb, 0)
                    if mm in (MM_O + 1, MM_O + 2):
                        ada_times_c(fb + Q_GF, mm - MM_O - 1)
                    if mm == 2 * MM_O:
                        hidden(fb, 1)
                    if last and mm > 2 * MM_O and mm % 2 == 0:
                        square_y2((mm - 2 * MM_O) // 2 - 1)
                if last:
                    square_y2(CG - 1)

            mlp_block(0, first=True)
            with act.Fori(1, FBS - 1) as fb:
                mlp_block(fb)
            mlp_block(FBS - 1, last=True)

        @block.vector
        def _(dve):
            def split_lo(m, n, view=slice(0, 2048)):
                dve.wait_ge(hi_done, m + 1)
                dve.wait_ge(w_used, m - 1)
                dve.tensor_tensor(w_lo[n][:, view], w_raw[n][:, view], w_hi[n][:, view].bitcast(F32), ALU.subtract)\
                    .then_inc(lo_done, 1)


            def evict_group(r, scaled):
                for b in range(1, TILES, 2):
                    if b < TILES - 1:
                        dve.wait_ge(tile_sum, r * (TILES - 1) + b + 1)
                    else:
                        dve.wait_ge(w_used, r * MM_G + MM_G)
                    if scaled and b == QB:
                        dve.tensor_scalar(grp[:, b, :], bank[b][:, :], FOX_DIM ** -0.5, None, ALU.mult)\
                            .then_inc(ev_dve, 1)
                    else:
                        dve.tensor_copy(grp[:, b, :], bank[b][:, :]).then_inc(ev_dve, 1)

            def fox_tiles_free(f):
                dve.wait_ge(fox_qk, 8 * f + 8)
                dve.wait_ge(fox_v_tr, 2 * f + 2)

            def gla_tiles_free(h):
                dve.drain()
                dve.wait_ge(gla_o, 2 * h + 2)
                dve.wait_ge(gla_v_tr, 2 * h + 2)
                dve.wait_ge(gla_sig_e, h + 1)

            def ada_reduce(q, u, b=0, used=None):
                if u == 0:
                    dve.wait_ge(ada_sum, q if used is None else used)
                dve.wait_ge(ada_mul[u], q + 1)
                dve.tensor_reduce(acc[b][:, u * P:(u + 1) * P], (ada0, ada1)[b][u][:, :, :].rearrange("p k n -> p n k"),
                                  AX_X, ALU.add).then_inc(ada_acc[u], 1)

            def mod_columns(q, k, dst, c_scale, c_shift, c_gain):
                dve.wait_ge(ada_sum, q + 1)
                dve.tensor_scalar(mod_a[:, bass.ds(k, 1)], dst[:, 0:1], cols_a[:, bass.ds(k + c_scale, 1)],
                                  cols_a[:, bass.ds(k + c_gain, 1)], ALU.add, ALU.mult)
                dve.tensor_tensor(mod_b[:, bass.ds(k, 1)], dst[:, 1:2], cols_a[:, bass.ds(k + c_shift, 1)], ALU.add)\
                    .then_inc(ada_col, 1)

            def gate_row(q, k, src, k0=0):
                dve.wait_ge(bg_in, 32 * (k + k0 + 1))
                dve.wait_ge(ada_sum, q + 1)
                part = gg[:, bass.ds(k * 2 * P, 2 * P)]
                dve.tensor_tensor(part, src[:, 0:2 * P], bg_bc[:, 0, :], ALU.add)
                dve.drain()
                dve.tensor_tensor(part, part, bg_bc[:, 1, :], ALU.mult).then_inc(ada_col, 1)

            ADA_SUM = {7: (0, 0), 9: (0, 1), 16: (1, 0), 18: (1, 1), 27: (2, 0), 30: (2, 1)}
            ADA_SUM_GLA = {7: (0, 0), 8: (0, 1), 16: (1, 0), 17: (1, 1), 28: (2, 0), 29: (2, 1)}
            F_COL = {14: 0, 23: 1, 31: 2}

            def fox_slot(s, f):
                if s % 3 == 0 and s // 3 < 8:
                    j = s // 3
                    n = (j % TB + 1) * P
                    diag = slice(n - P, n)
                    if j:
                        dve.wait_ge(fox_exp, 8 * f + j)
                    dve.wait_ge(fox_bias_ready, 8 * f + j + 1)
                    dve.wait_ge(fox_qk, 8 * f + j + 1)
                    dve.tensor_tensor(bias[:, diag], bias[:, diag], causal[:, :], ALU.min)
                    dve.drain()
                    dve.tensor_tensor_reduce(logit[:, 0:n], BA[:, 0:n], bias[:, 0:n], 1.0, MASKED,
                                             ALU.add, ALU.max, row_max[:, j:j + 1])
                    dve.drain()
                    dve.tensor_scalar(neg_max[:, j:j + 1], row_max[:, j:j + 1], -1.0, None, ALU.mult)\
                        .then_inc(fox_max, 1)
                if s in F_COL:
                    k = 3 * f + F_COL[s]
                    mod_columns(k + Q_FOX, k, BA, C_SCF, C_SHF, C_GPRE2)
                if s % 3 == 1 and 4 <= s <= 25:
                    j = (s - 4) // 3
                    dve.wait_ge(fox_exp, 8 * f + j + 1)
                    dve.reciprocal(row_inv[:, j:j + 1], row_sum[:, j:j + 1])
                    dve.drain()
                    dve.wait_ge(fox_pv, 9 * f + j + 1)
                    if j:
                        fox_store(f, j - 1)
                    dve.tensor_scalar(f_o[:, :], BB[:, 0:P], row_inv[:, j:j + 1], None, ALU.mult).then_inc(fox_out, 1)
                    dve.drain()
                    dve.tensor_tensor_reduce(f_junk[:, :], f_o[:, :], f_o[:, :], 1.0 / FOX_DIM, EPS, ALU.mult, ALU.add,
                                             f_ms[:, j:j + 1]).then_inc(fox_ss, 1)
                if s % 3 == 0 and 6 <= s <= 27:
                    j = s // 3 - 2
                    dve.wait_ge(fox_rstd, 8 * f + j + 1)
                    dve.tensor_scalar(f_o[:, :], f_o[:, :], f_r[:, j:j + 1], None, ALU.mult).then_inc(fox_norm, 1)
                if s == 28:
                    dve.wait_ge(fox_pv, 9 * f + 9)
                    fox_store(f, 7).then_inc(fox_out, 1)
                    dve.drain()

            def fox_store(f, j):
                i, head = j % TB, 2 * f + j // TB
                return dve.tensor_scalar(cat[:, bass.ds(head, 1), i * P:i * P + P].rearrange("p o n -> p (o n)"),
                                         BB[:, P:2 * P], cols_b[:, bass.ds(head + B_GFOX, 1)], None, ALU.mult)

            SIG_AT, SIG_MUL = (14, 21), 22

            def gla_slot(s, h, ada, last_head=False):
                if s == 0:
                    dve.drain()
                    dve.wait_ge(gla_z, h + 1)
                    dve.tensor_scalar(g_z[:, :], BA[:, :], cols_b[:, bass.ds(h + B_A2, 1)], None, ALU.add)
                    dve.drain()
                    dve.scalar_tensor_tensor(g_e[:, :], g_z[:, :], -1.0, g_z[:, :], ALU.mult, ALU.min).then_inc(gla_abs, 1)
                if s == 3:
                    dve.wait_ge(gla_ln, h + 1)
                    dve.scalar_tensor_tensor(g_z[:, :], g_z[:, :], 0.0, g_e[:, :], ALU.min, ALU.subtract)
                    dve.drain()
                    dve.tensor_tensor_scan(g_cum[:, :, :].rearrange("p n c -> p (n c)"), chunk_on[:, :], g_z[:, :],
                                           0.0, ALU.mult, ALU.add)
                    dve.drain()
                    dve.tensor_tensor(g_dif[:, :, :], g_cum[:, :, CHUNK - 1:CHUNK].to_broadcast([P, NCH, CHUNK]),
                                      g_cum[:, :, :], ALU.subtract).then_inc(gla_cum, 1)
                if s == 6:
                    dve.wait_ge(gla_decay, h + 1)
                    dve.tensor_tensor(g_e[:, :], grp[:, GK, :], g_dif[:, :, :].rearrange("p n c -> p (n c)"),
                                      ALU.mult).then_inc(gla_kd, 1)
                if s == 7:
                    dve.wait_ge(gla_sig_e, h + 1)
                    dve.tensor_scalar(sig, sig, 1.0, None, ALU.add)
                if s in SIG_AT:
                    dve.drain()
                    dve.reciprocal(sig[:, SIG_AT.index(s), :], sig[:, SIG_AT.index(s), :])
                if s == SIG_MUL:
                    dve.drain()
                    dve.tensor_tensor(sig, sig, grp[:, GR0:GR1 + 1, :], ALU.mult)
                if s == 12:
                    mod_columns(ada, h + 3 * FOX_GROUPS, BB, C_SCF, C_SHF, C_GPRE2)
                if s in (10, 13):
                    n0 = 4 * (s == 13)
                    dve.wait_ge(gla_u, 2 * h + 1 + (s == 13))
                    for n in range(n0, n0 + 4):
                        u = (BA, BB)[n % 2][:, (n - n0) // 2 * GLA_DV:((n - n0) // 2 + 1) * GLA_DV]
                        if n == 0:
                            last = dve.tensor_copy(states[:, 0, :], u)
                        else:
                            last = dve.scalar_tensor_tensor(states[:, n, :], states[:, n - 1, :],
                                                            decay[:, n:n + 1], u, ALU.mult, ALU.add)
                        if n % 4 < 3:
                            dve.drain()
                    last.then_inc(gla_state, 1)
                    dve.drain()
                if s == 18:
                    dve.wait_ge(gla_o_tok, 2 * h + 2)
                    for t in range(TB):
                        last = dve.tensor_tensor_reduce(g_junk[:, :], g_o[:, t, :], g_o[:, t, :], 1.0 / GLA_DV, EPS,
                                                        ALU.mult, ALU.add, ms[:, t:t + 1])
                        if t < TB - 1:
                            dve.drain()
                    last.then_inc(gla_ss, 1)
                if s == 20:
                    dve.wait_ge(gla_rstd, h + 1)
                    for t in range(TB):
                        last = dve.tensor_scalar(g_o[:, t, :], g_o[:, t, :], rstd[:, t:t + 1], None, ALU.mult)
                    last.then_inc(gla_norm, 1)
                    if not last_head:
                        gate_row(ada + 1, h * 2, BA)
                if s in (24, 25):
                    half = s - 24
                    dve.drain()
                    dve.wait_ge(gla_o_tr, 2 * h + half + 1)
                    row = cat[:, bass.ds(h * 2 + (FOX_HEADS + half), 1), :].rearrange("p o n -> p (o n)")
                    dve.scalar_tensor_tensor(row, (BA, BB)[half][:, :], cols_b[:, bass.ds(h * 2 + (B_GGLA + half), 1)],
                                             sig[:, half, :], ALU.mult, ALU.mult).then_inc(gla_cat, 1)
                if s == 31 and not last_head:
                    gate_row(ada + 2, h * 2 + 1, BA)

            dve.wait_ge(ce_ready, 1)
            dve.tensor_scalar(c_act[:, :], c_act[:, :], 1.0, None, ALU.add)
            dve.drain()
            dve.reciprocal(c_act[:, :], c_act[:, :])
            dve.drain()
            dve.tensor_tensor(c_act[:, :], c_act[:, :], BB[:, 0:KT], ALU.mult).then_inc(c_ready, 1)
            for q in range(2):
                ada_reduce(q, 0, q, 0)
                ada_reduce(q, 1, q)
            dve.wait_ge(rows_tr, 1)
            dve.tensor_copy(cols_a[:, :], BA[:, 0:6 * KT])
            dve.tensor_copy(cols_b[:, :], BA[:, 128:148])
            dve.drain()
            for col in (C_SCM, C_SCF):
                last = dve.tensor_scalar(cols_a[:, col:col + KT], cols_a[:, col:col + KT], 1.0, None, ALU.add)
            last.then_inc(cols_ready, 1)
            for t in range(TB):
                dve.wait_ge(x_rstd, t + 1)
                dve.tensor_scalar(x_raw[:, t, :], x_raw[:, t, :], rstd[:, t:t + 1], None, ALU.mult)\
                    .then_inc(xn_ready, 1)
            for k in range(1, KT, 2):
                dve.wait_ge(x_tr, k + 1)
                dve.tensor_copy(xn_t[:, k, :], bank[k % TILES][:, :]).then_inc(xt_dve, 1)

            def modulated_lo(k, n):
                dve.wait_ge(mod_hi, n + 1)
                dve.tensor_tensor(in_lo[:, k, :], in_tmp[:, k, :], in_hi[:, k, :].bitcast(F32),
                                  ALU.subtract).then_inc(mod_lo, 1)

            def first_lo(m):
                dve.wait_ge(hi_done, m + 1)
                dve.tensor_tensor(w_lo[m][:, NARROW], w_raw[m][:, NARROW], w_hi[m][:, NARROW].bitcast(F32),
                                  ALU.subtract).then_inc(lo_done, 1)

            def mod_columns_m(q):
                mod_columns(q, q, BA[:, 0:2], C_SCM, C_SHM, C_GPRE)

            mod_columns_m(0)
            dve.wait_ge(wm_hid, 1)
            dve.tensor_tensor(wm_lo[:, :, :], wm_raw[:, :, :], wm_hi[:, :, :].bitcast(F32), ALU.subtract)\
                .then_inc(wm_lod, 1)
            mod_columns_m(1)
            first_lo(0)
            modulated_lo(0, 0)
            for q in range(2, KT):
                ada_reduce(q, 0, q % 2, q - 1)
                ada_reduce(q, 1, q % 2)
                mod_columns_m(q)
                if q == 2:
                    first_lo(1)
                modulated_lo(q - 1, q - 1)
                if q % 2 == 0 and q >= 4:
                    split_lo(q // 2, q // 2 % 2, NARROW)
            modulated_lo(KT - 1, KT - 1)
            dve.wait_ge(misc_sum, 1)
            dve.wait_ge(bfg_in, 16)
            dve.tensor_scalar(f_z[32:40, :], BB[32:40, :], b_fg[32:40, 0:1], None, ALU.add)
            dve.tensor_copy(ga_t[:, :], BB[0:RANK, :])
            dve.drain()
            dve.scalar_tensor_tensor(f_a[32:40, :], f_z[32:40, :], -1.0, f_z[32:40, :], ALU.mult, ALU.min)\
                .then_inc(fz_abs, 1)
            dve.wait_ge(fz_ln, 1)
            dve.scalar_tensor_tensor(f_a[32:40, :], f_z[32:40, :], 0.0, f_a[32:40, :], ALU.min, ALU.subtract)
            dve.drain()
            dve.wait_ge(consts, 2)
            dve.tensor_tensor_scan(f_z[32:40, :], ones[32:40, 0:1].to_broadcast([8, SEQ]), f_a[32:40, :], 0.0,
                                   ALU.mult, ALU.add).then_inc(cum_ready, 1)
            split_lo(MM_G, 0, NARROW)
            evict_group(0, True)

            def cat_half(k):
                dve.wait_ge(cat_hi, k + 1)
                dve.tensor_tensor(in_lo[:, k, :], cat[:, k, :], in_hi[:, k, :].bitcast(F32),
                                  ALU.subtract).then_inc(cat_lo, 1)

            CAT_AT = {4 * (k // 2 + 1) + 2 + k % 2: k for k in range(12)}

            def group(r, work, q, ada_sum, last=False):
                for s in range(4 * MM_G):
                    work(s)
                    if last and s in CAT_AT:
                        cat_half(CAT_AT[s])
                    if s in ada_sum:
                        ada_reduce(q + ada_sum[s][0], ada_sum[s][1])
                    if s % 4 == 0 and (s // 4 + 1 < MM_G or not last):
                        split_lo(r * MM_G + (s // 4 + 1), (s // 4 + 1) % 2, NARROW)

            with dve.Fori(1, FOX_GROUPS) as r:
                group(r, lambda s: fox_slot(s, r - 1), 3 * r + (Q_FOX - 3), ADA_SUM)
                fox_tiles_free(r - 1)
                evict_group(r, True)
            group(FOX_GROUPS, lambda s: fox_slot(s, FOX_GROUPS - 1), Q_GLA - 3, ADA_SUM)
            fox_tiles_free(FOX_GROUPS - 1)
            evict_group(FOX_GROUPS, False)

            def gla_group(h, last=False):
                group(h + (FOX_GROUPS + 1), lambda s: gla_slot(s, h, h * 3 + Q_GLA), h * 3 + Q_GLA, ADA_SUM_GLA, last)
                if last:
                    split_lo(M_OUT, 0)
                gla_tiles_free(h)
                evict_group(h + (FOX_GROUPS + 1), False)

            with dve.Fori(0, GLA_HEADS - 2) as h:
                gla_group(h)
            gla_group(GLA_HEADS - 2, last=True)

            for k in (KT - 4, KT - 3):
                cat_half(k)
            for s in range(2 * KT):
                gla_slot(s, GLA_HEADS - 1, Q_GF - 3, True)
                if s in (7, 8):
                    ada_reduce(Q_GF - 3, s - 7)
                if s % 8 == 2 and s // 8 + 1 < MM_O:
                    split_lo(M_OUT + s // 8 + 1, (s // 8 + 1) % 2)
                if s == 27:
                    cat_half(KT - 2)
                    cat_half(KT - 1)

            def gain_y(cg, t):
                dve.wait_ge(y_sq, cg * TB + t + 1)
                cols = slice(cg * 512, cg * 512 + 512)
                dve.tensor_tensor(y[:, t, cols], bank[4 * (cg % 2) + t][:, :], gg[:, cols], ALU.mult).then_inc(y_mul, 1)

            def scale_x1(t):
                dve.wait_ge(x1_rstd, t + 1)
                dve.tensor_scalar(y[:, t, :], x_res[:, t, :], rstd[:, 4 + t:5 + t], None, ALU.mult)\
                    .then_inc(xn2_dve, 1)

            for cg in range(CG):
                if cg:
                    for mm in range(2, MM_O):
                        split_lo(M_OUT + cg * MM_O + mm, mm % 2)
                    if cg < 3:
                        ada_reduce(Q_GF - 3 + cg, 0)
                        ada_reduce(Q_GF - 3 + cg, 1)
                        gate_row(Q_GF - 3 + cg, KT // 2 - 3 + cg, bank[(3, 7)[cg - 1]])
                        dve.drain()
                if cg < CG - 1:
                    split_lo(M_OUT + cg * MM_O + MM_O, 0)
                    for t in range(TB):
                        gain_y(cg, t)
                    split_lo(M_OUT + cg * MM_O + MM_O + 1, 1)
            for t in range(TB):
                dve.wait_ge(y_sq, (CG - 1) * TB + t + 1)
                dve.tensor_reduce(ss4[:, t:t + 1], ss[:, t * CG:(t + 1) * CG], AX_X, ALU.add).then_inc(y_gate, 1)
                gain_y(CG - 1, t)
                dve.drain()
                dve.wait_ge(xres_in[t], 16)
                dve.wait_ge(y_rstd, t + 1)
                for half in range(2 if t == TB - 1 else 1):
                    cols = slice(half * D // 2, (half + 1) * D // 2) if t == TB - 1 else slice(0, D)
                    dve.scalar_tensor_tensor(x_res[:, t, cols], y[:, t, cols], rstd[:, t:t + 1], x_res[:, t, cols],
                                             ALU.mult, ALU.add).then_inc(x1_ready, 1)
                if t >= 2:
                    scale_x1(t - 1)
            dve.wait_ge(x1_ss, TB + 1)
            dve.tensor_reduce(ss_x[:, TB + 1:TB + 2], ss_x[:, TB - 1:TB + 1], AX_X, ALU.add).then_inc(x1_sq, 1)
            split_lo(M_MLP, 0)
            scale_x1(TB - 1)
            for k in range(KT):
                dve.wait_ge(x_tr, KT + k + 1)
                dve.tensor_scalar(in_tmp[:, k, :], bank[4 + k % 4][:, :], mod_a[:, k:k + 1], mod_b[:, k:k + 1],
                                  ALU.mult, ALU.add).then_inc(mod_tmp, 1)
                if k:
                    modulated_lo(k - 1, KT + k - 1)
                if k in (2, 8, 12):
                    split_lo(M_MLP + max(k // 4, 1), max(k // 4, 1) % 2)
            modulated_lo(KT - 1, 2 * KT - 1)

            def hidden(fb, half):
                def square(b):
                    dve.wait_ge(h_relu, fb * FT + half * 4 + b + 1)
                    dve.tensor_tensor(hid_tmp[:, half * 4 + b, :], hid_tmp[:, half * 4 + b, :],
                                      hid_tmp[:, half * 4 + b, :], ALU.mult).then_inc(h_sq, 1)

                def lo(b):
                    dve.wait_ge(h_hi, fb * FT + half * 4 + b + 1)
                    dve.tensor_tensor(hid_lo[:, half * 4 + b, :], hid_tmp[:, half * 4 + b, :],
                                      hid_hi[:, half * 4 + b, :].bitcast(F32), ALU.subtract).then_inc(h_lo, 1)

                for b in range(4):
                    square(b)
                mm = (half + 1) * MM_O + 1
                split_lo(M_MLP + fb * MM_F + mm, mm % 2)
                for b in range(4):
                    lo(b)

            def add_y2(fb, cg):
                for t in range(TB):
                    if t < TB - 1:
                        dve.wait_ge(y2_sum, (fb * CG + cg) * (TB - 1) + t + 1)
                    else:
                        dve.wait_ge(w_used, M_MLP + fb * MM_F + 2 * MM_O + cg * 2 + 2)
                    part = y[:, t, cg * 512:cg * 512 + 512]
                    dve.tensor_tensor(part, bank[4 + t][:, :], part, ALU.add).then_inc(y2_add, 1)

            def mlp_block(fb, first=False, last=False):
                for mm in range(MM_O if first else 1, MM_F):
                    if mm not in (MM_O + 1, 2 * MM_O + 1):
                        split_lo(M_MLP + fb * MM_F + mm, mm % 2)
                    if first and mm == MM_O:
                        dve.memset(y[:, :, :], 0.0).then_inc(y2_add, 1)
                        dve.drain()
                    if mm == MM_O:
                        hidden(fb, 0)
                    if mm == MM_O + 3:
                        ada_reduce(fb + Q_GF, 0)
                        ada_reduce(fb + Q_GF, 1)
                    if mm == 2 * MM_O - 1:
                        gate_row(fb + Q_GF, fb, bank[7], KT // 2)
                    if mm == 2 * MM_O:
                        hidden(fb, 1)
                    if mm > 2 * MM_O and mm % 2 == 0:
                        add_y2(fb, (mm - 2 * MM_O) // 2 - 1)
                if not last:
                    split_lo(M_MLP + fb * MM_F + MM_F, 0)
                    add_y2(fb, CG - 1)

            mlp_block(0, first=True)
            with dve.Fori(1, FBS - 1) as fb:
                mlp_block(fb)
            mlp_block(FBS - 1, last=True)
            for t in range(TB):
                if t < TB - 1:
                    dve.wait_ge(y2_sum, (FBS * CG - 1) * (TB - 1) + t + 1)
                else:
                    dve.wait_ge(w_used, M_MLP + FBS * MM_F)
                part = y[:, t, (CG - 1) * 512:CG * 512]
                dve.tensor_tensor(part, bank[4 + t][:, :], part, ALU.add).then_inc(y2_add, 1)
                dve.wait_ge(o_sq, (CG - 1) * TB + t + 1)
                dve.tensor_reduce(ss4[:, t:t + 1], ss[:, t * CG:(t + 1) * CG], AX_X, ALU.add).then_inc(o_ss, 1)
                dve.tensor_tensor(part, part, gg[:, (CG - 1) * 512:CG * 512], ALU.mult)
                dve.drain()
                dve.wait_ge(o_mul, CG - 1)
                dve.wait_ge(x1_in[t], 16)
                dve.wait_ge(o_rstd, t + 1)
                for half in range(2 if t == TB - 1 else 1):
                    cols = slice(half * D // 2, (half + 1) * D // 2) if t == TB - 1 else slice(0, D)
                    dve.scalar_tensor_tensor(x1_end[:, t, cols], y[:, t, cols], rstd[:, t:t + 1], x1_end[:, t, cols],
                                             ALU.mult, ALU.add).then_inc(o_ready, 1)

        @block.gpsimd
        def _(pool):
            def inverse_root(dst, mean, total, n):
                pool.tensor_scalar(mean, total, 1.0 / n, EPS, ALU.mult, ALU.add)
                pool.drain()
                return pool.tensor_tensor(dst, mean, neg_half[:, 0:mean.shape[1]], ALU.pow)

            def ada_second(q, b=0, arrived=None):
                pool.wait_ge(ada_in[b][1], 16 * (q - Q_FOX + KT // 2 + 1) if arrived is None else arrived)
                unit = (ada0, ada1)[b][1]
                pool.tensor_tensor(unit[:, :, :], unit[:, :, :],
                                   c_act[:, :].rearrange("p (k o) -> p k o", o=1).to_broadcast([P, KT, P]), ALU.mult)\
                    .then_inc(ada_mul[1], 1)

            pool.memset(ident[:, :], 0.0)
            pool.memset(ones[:, :], 1.0)
            pool.drain()
            pool.affine_select(out=ident[:, :], in_=ident[:, :], compare_op=ALU.not_equal, fill=1.0,
                               base=0, pattern=[[-1, P]], channel_multiplier=1).then_inc(consts, 1)
            pool.memset(wm_raw[:, :, :], 0.0).then_inc(wm_zero, 1)
            pool.memset(neg_half[:, :], -0.5)
            pool.memset(causal[:, :], -MASKED)
            pool.memset(chunk_on[:, :], 1.0)
            pool.drain()
            pool.affine_select(out=causal[:, :], in_=causal[:, :], compare_op=ALU.is_ge, fill=MASKED,
                               base=0, pattern=[[-1, P]], channel_multiplier=1)
            pool.memset(chunk_on[:, :].rearrange("p (n c) -> p n c", c=CHUNK)[:, :, 0:1], 0.0).then_inc(consts, 1)
            pool.wait_ge(c_ready, 1)
            ada_second(0, 0, 16)
            ada_second(1, 1, 16)
            for t in range(TB):
                pool.wait_ge(x_ss, t + 1)
                inverse_root(rstd[:, t:t + 1], ms[:, t:t + 1], ss[:, t:t + 1], D).then_inc(x_rstd, 1)
            for q in range(2, KT):
                ada_second(q, q % 2, 16 * (q // 2 + 1))

            def x1_root(t, n):
                if t < TB - 1:
                    pool.wait_ge(x1_ss, t + 1)
                inverse_root(rstd[:, 4 + t:5 + t], ms[:, 4 + t:5 + t], ss_x[:, n:n + 1], D).then_inc(x1_rstd, 1)

            def fox(f):
                MUL = {5: 0, 14: 1, 23: 2}
                for s in range(32):
                    if s % 3 == 1 and 4 <= s <= 25:
                        j = (s - 4) // 3
                        pool.wait_ge(fox_ss, 8 * f + j + 1)
                        pool.tensor_tensor(f_r[:, j:j + 1], f_ms[:, j:j + 1], neg_half[:, 0:1], ALU.pow)\
                            .then_inc(fox_rstd, 1)
                    if s in MUL:
                        ada_second(3 * f + (MUL[s] + Q_FOX))

            def gla(h, q, last_head=False):
                ada_second(q)
                if not last_head:
                    ada_second(q + 1)
                pool.wait_ge(gla_ss, h + 1)
                pool.tensor_tensor(rstd[:, 0:TB], ms[:, 0:TB], neg_half[:, 0:TB], ALU.pow).then_inc(gla_rstd, 1)
                if not last_head:
                    ada_second(q + 2)

            with pool.Fori(0, FOX_GROUPS - 1) as f:
                fox(f)
            fox(FOX_GROUPS - 1)
            with pool.Fori(0, GLA_HEADS - 1) as h:
                gla(h, h * 3 + Q_GLA)
            gla(GLA_HEADS - 1, Q_GF - 3, True)
            ada_second(Q_GF - 2)
            ada_second(Q_GF - 1)
            for t in range(TB):
                pool.wait_ge(y_gate, t + 1)
                inverse_root(rstd[:, t:t + 1], ms[:, t:t + 1], ss4[:, t:t + 1], D).then_inc(y_rstd, 1)
                if t:
                    x1_root(t - 1, t - 1)
            pool.wait_ge(x1_sq, 1)
            x1_root(TB - 1, TB + 1)
            with pool.Fori(0, FBS) as fb:
                ada_second(fb + Q_GF)
            pool.wait_ge(ada_col, Q_GF + FBS)
            for cg in range(CG - 1):
                pool.wait_ge(o_sq, cg * TB + TB)
                cols = slice(cg * 512, cg * 512 + 512)
                pool.tensor_tensor(y[:, :, cols], y[:, :, cols],
                                   gg[:, cols].rearrange("p (o n) -> p o n", o=1).to_broadcast([P, TB, 512]),
                                   ALU.mult).then_inc(o_mul, 1)
            for t in range(TB):
                pool.wait_ge(o_ss, t + 1)
                inverse_root(rstd[:, t:t + 1], ms[:, t:t + 1], ss4[:, t:t + 1], D).then_inc(o_rstd, 1)


_INS = ["x", "c", "w_ada", "b_ada", "g_pre_mix", "g_post_mix", "w_in", "b_fgate", "w_gla_a2", "b_gla_a2",
        "g_fox_out", "g_gla_out", "w_out", "g_pre_mlp", "g_post_mlp", "w_mlp_in", "w_mlp_out"]


def kernel(**inputs):
    import concourse.bacc as bacc
    from concourse.bass_utils import run_bass_kernel_spmd

    nc = bacc.Bacc("TRN2", target_bir_lowering=False, num_devices=1)
    arrays, args = {}, []
    for name in _INS:
        a = np.ascontiguousarray(inputs[name])
        arrays[f"in_{name}"] = a
        args.append(nc.dram_tensor(f"in_{name}", a.shape, mybir.dt.from_np(a.dtype), kind="ExternalInput").ap())
    shape = inputs["x"].shape
    args.append(nc.dram_tensor("out", shape, F32, kind="ExternalOutput").ap())
    build_block(nc, *args)
    r = run_bass_kernel_spmd(nc, [arrays], core_ids=[0])
    return r.results[0]["out"]
```
